# Optimizing a Trainium2 kernel written in Bass

```python
import jax, jax.numpy as jnp
from jax import lax
import numpy as np

D_MODEL = 2048
BATCH = 1
SEQ = 512
DEPTH = 1

HEAD_DIM = 64
N_Q_HEADS = 16
N_KV_HEADS = 4
Q_PER_KV = N_Q_HEADS // N_KV_HEADS
ATTN_WIDTH = N_Q_HEADS * HEAD_DIM
KV_WIDTH = N_KV_HEADS * HEAD_DIM
WINDOW = 128
BLOCK = 128
ROPE_THETA = 500000.0
ROT_DIM = HEAD_DIM // 4

CONV_WIDTH = D_MODEL // 2
CONV_K = 3

N_MEM = 256
X_HEADS = 4
X_HEAD_DIM = 128
X_WIDTH = X_HEADS * X_HEAD_DIM

D_FF = -(-8 * D_MODEL // (3 * 256)) * 256

IN_SIZES = (ATTN_WIDTH, KV_WIDTH, KV_WIDTH, CONV_WIDTH, CONV_WIDTH, CONV_WIDTH, D_MODEL, D_MODEL)
IN_WIDTH = sum(IN_SIZES)

EPS = 1e-6

kernel_name = "hybrid_swa_sink_shortconv_gated_merge"

def rms_norm(x, g):
    xf = x.astype(jnp.float32)
    y = xf * lax.rsqrt(jnp.mean(xf * xf, axis=-1, keepdims=True) + EPS)
    return (y * g.astype(jnp.float32)).astype(x.dtype)

def partial_rope(t, pos):
    half = ROT_DIM // 2
    inv_freq = ROPE_THETA ** (-jnp.arange(0, ROT_DIM, 2, dtype=jnp.float32) / ROT_DIM)
    ang = pos.astype(jnp.float32)[:, None] * inv_freq[None, :]
    cos = jnp.cos(ang)[None, :, None, :]
    sin = jnp.sin(ang)[None, :, None, :]
    tr = t[..., :ROT_DIM].astype(jnp.float32)
    t1, t2 = tr[..., :half], tr[..., half:]
    rot = jnp.concatenate([t1 * cos - t2 * sin, t2 * cos + t1 * sin], axis=-1).astype(t.dtype)
    return jnp.concatenate([rot, t[..., ROT_DIM:]], axis=-1)

def sliding_window_sink_attention(q, k, v, sinks):
    B, S = q.shape[0], q.shape[1]
    nb = S // BLOCK
    qb = q.reshape(B, nb, BLOCK, N_KV_HEADS, Q_PER_KV, HEAD_DIM)

    def with_prev(t):
        tb = t.reshape(B, nb, BLOCK, N_KV_HEADS, HEAD_DIM)
        prev = jnp.pad(tb[:, :-1], ((0, 0), (1, 0), (0, 0), (0, 0), (0, 0)))
        return jnp.concatenate([prev, tb], axis=2)

    kb, vb = with_prev(k), with_prev(v)
    scale = HEAD_DIM ** -0.5
    s = jnp.einsum('bnqkgd,bnckd->bkgnqc', qb, kb).astype(jnp.float32) * scale
    qi = jnp.arange(BLOCK)[:, None]
    c = jnp.arange(2 * BLOCK)[None, :]
    rel = qi + BLOCK - c
    band = (rel >= 0) & (rel < WINDOW)
    not_first = (jnp.arange(nb) > 0)[:, None, None]
    valid = band[None] & (not_first | (c >= BLOCK)[None])
    s = jnp.where(valid, s, -jnp.inf)
    sink = sinks.astype(jnp.float32).reshape(N_KV_HEADS, Q_PER_KV)[None, :, :, None, None, None]
    m = jnp.maximum(jnp.max(s, axis=-1, keepdims=True), sink)
    p = jnp.exp(s - m)
    denom = jnp.sum(p, axis=-1, keepdims=True) + jnp.exp(sink - m)
    w = (p / denom).astype(v.dtype)
    o = jnp.einsum('bkgnqc,bnckd->bnqkgd', w, vb)
    return o.reshape(B, S, ATTN_WIDTH)

def gated_short_conv(u, b_gate, c_gate, conv_w):
    S = u.shape[1]
    v = c_gate * u
    vp = jnp.pad(v, ((0, 0), (CONV_K - 1, 0), (0, 0)))
    y = conv_w[0] * vp[:, 0:S]
    for tap in range(1, CONV_K):
        y = y + conv_w[tap] * vp[:, tap:tap + S]
    return b_gate * y

def memory_cross_attention(h, mem_n, w_xq, w_xkv, w_xo):
    B, S = h.shape[0], h.shape[1]
    q = (h @ w_xq).reshape(B, S, X_HEADS, X_HEAD_DIM)
    kv = mem_n @ w_xkv
    k = kv[..., :X_WIDTH].reshape(B, -1, X_HEADS, X_HEAD_DIM)
    v = kv[..., X_WIDTH:].reshape(B, -1, X_HEADS, X_HEAD_DIM)
    s = jnp.einsum('bshd,bmhd->bhsm', q, k).astype(jnp.float32) * (X_HEAD_DIM ** -0.5)
    p = jax.nn.softmax(s, axis=-1).astype(v.dtype)
    o = jnp.einsum('bhsm,bmhd->bshd', p, v).reshape(B, S, X_WIDTH)
    return o @ w_xo

def swiglu(h, w_gate_up, w_down):
    gu = h @ w_gate_up
    g, u = gu[..., :D_FF], gu[..., D_FF:]
    return (jax.nn.silu(g) * u) @ w_down

def setup_inputs(seed: int = 0) -> dict:
    key = jax.random.key(seed)
    ks = jax.random.split(key, 20)
    f32 = jnp.float32

    def nrm(k, shape, scale):
        return jax.random.normal(k, shape, f32) * scale

    L, D = DEPTH, D_MODEL
    return {
        "x": nrm(ks[0], (BATCH, SEQ, D), 1.0),
        "mem": nrm(ks[1], (BATCH, N_MEM, D), 1.0),
        "g_mix": 1.0 + nrm(ks[2], (L, D), 0.02),
        "w_in": nrm(ks[3], (L, D, IN_WIDTH), D ** -0.5),
        "conv_w": nrm(ks[4], (L, CONV_K, CONV_WIDTH), CONV_K ** -0.5),
        "sinks": nrm(ks[5], (L, N_Q_HEADS), 0.5),
        "w_attn_o": nrm(ks[6], (L, ATTN_WIDTH, D), ATTN_WIDTH ** -0.5),
        "w_conv_o": nrm(ks[7], (L, CONV_WIDTH, D), CONV_WIDTH ** -0.5),
        "w_out": nrm(ks[8], (L, D, D), D ** -0.5),
        "g_xattn": 1.0 + nrm(ks[9], (L, D), 0.02),
        "g_mem": 1.0 + nrm(ks[10], (L, D), 0.02),
        "w_xq": nrm(ks[11], (L, D, X_WIDTH), D ** -0.5),
        "w_xkv": nrm(ks[12], (L, D, 2 * X_WIDTH), D ** -0.5),
        "w_xo": nrm(ks[13], (L, X_WIDTH, D), X_WIDTH ** -0.5),
        "g_ffn": 1.0 + nrm(ks[14], (L, D), 0.02),
        "w_gate_up": nrm(ks[15], (L, D, 2 * D_FF), D ** -0.5),
        "w_down": nrm(ks[16], (L, D_FF, D), D_FF ** -0.5),
        "g_final": 1.0 + nrm(ks[17], (D,), 0.02),
    }

def reference(x, mem, g_mix, w_in, conv_w, sinks, w_attn_o, w_conv_o, w_out,
              g_xattn, g_mem, w_xq, w_xkv, w_xo, g_ffn, w_gate_up, w_down, g_final):
    B, S = x.shape[0], x.shape[1]
    pos = jnp.arange(S, dtype=jnp.int32)
    h = x
    for l in range(DEPTH):
        n = rms_norm(h, g_mix[l])
        z = n @ w_in[l]
        parts = []
        off = 0
        for size in IN_SIZES:
            parts.append(z[..., off:off + size])
            off += size
        q, k, v, cb, cc, ch, ga, gc = parts
        q = partial_rope(q.reshape(B, S, N_Q_HEADS, HEAD_DIM), pos)
        k = partial_rope(k.reshape(B, S, N_KV_HEADS, HEAD_DIM), pos)
        v = v.reshape(B, S, N_KV_HEADS, HEAD_DIM)
        y_attn = sliding_window_sink_attention(q, k, v, sinks[l]) @ w_attn_o[l]
        y_conv = gated_short_conv(ch, cb, cc, conv_w[l]) @ w_conv_o[l]
        merged = jax.nn.sigmoid(ga) * y_attn + jax.nn.sigmoid(gc) * y_conv
        h = h + merged @ w_out[l]
        mem_n = rms_norm(mem, g_mem[l])
        h = h + memory_cross_attention(rms_norm(h, g_xattn[l]), mem_n, w_xq[l], w_xkv[l], w_xo[l])
        h = h + swiglu(rms_norm(h, g_ffn[l]), w_gate_up[l], w_down[l])
    return rms_norm(h, g_final)


_drawn_inputs = setup_inputs


def setup_inputs(seed=0):
    import zlib

    import numpy as np

    out = dict(_drawn_inputs(seed))
    spreads = {}
    factors = {'g_mix': 2.914,
     'sinks': 64.0,
     'g_xattn': 8.0,
     'g_mem': 8.0,
     'g_ffn': 14.119,
     'g_final': 7.987}
    for name, (base, spread) in spreads.items():
        noise = np.random.default_rng([zlib.crc32(name.encode()), seed]).standard_normal(out[name].shape)
        drawn = base * np.exp(spread * noise) if base else spread * noise
        out[name] = __import__('jax').numpy.asarray(drawn.astype(out[name].dtype))
    for name, factor in factors.items():
        out[name] = (out[name] * factor).astype(out[name].dtype)
    return out
```

```python
from contextlib import ExitStack

import numpy as np

import concourse.bass as bass
from concourse import mybir

F32 = mybir.dt.float32
F32R = mybir.dt.float32r
ACT = mybir.ActivationFunctionType
ALU = mybir.AluOpType

P = 128
D = 2048
SEQ = 512
NMEM = 256
KT = D // P
TT = SEQ // P
MT = NMEM // P
HD = 64
NQ = 16
NKV = 4
PAIRS = NQ // 2
ROT = HD // 4
HALF = ROT // 2
THETA = 500000.0
CONV = D // 2
CT = CONV // P
TAPS = 3
XH = 4
XHD = 128
FF = -(-8 * D // (3 * 256)) * 256
FG = FF // 512
EPS = 1e-6
NEG = -3.0e38

Q0 = 0
K0 = NQ * HD
CB0 = K0 + 2 * NKV * HD
CC0 = CB0 + CONV
CH0 = CC0 + CONV
GA0 = CH0 + CONV
GC0 = GA0 + D

B_QKV = 0
B_CONV = B_QKV + 3 * KT
B_MERGE = B_CONV + 6 * KT
MERGE_BLOCKS = 2 * KT + 2 * CT
B_WOUT = B_MERGE + 4 * MERGE_BLOCKS
B_XQ = B_WOUT + 4 * KT
B_XK = B_XQ + KT
B_XV = B_XK + KT
B_XO = B_XV + KT
B_G0 = B_XO + 4 * XH
B_U0 = B_G0 + KT
B_FFN = B_U0 + KT
FFN_BLOCKS = 3 * KT
B_LAST = B_FFN + (FG - 1) * FFN_BLOCKS

G_QKV = 0
G_CONV = 3
G_MERGE = 9
G_WOUT = G_MERGE + 16
G_XQ = G_WOUT + 4
G_XK = G_XQ + 1
G_XV = G_XK + 1
G_XO = G_XV + 1
G_G0 = G_XO + 4
G_U0 = G_G0 + 1
G_FFN = G_U0 + 1
G_LAST = G_FFN + 6 * (FG - 1)

RAW = 4
SPL = 4
UNITS = PAIRS * TT


def rope_table():
    inv = (THETA ** (-np.arange(0, ROT, 2, dtype=np.float32) / np.float32(ROT))).astype(np.float32)
    ang = np.arange(SEQ, dtype=np.float32)[:, None] * inv[None, :]
    return np.concatenate([np.cos(ang), np.sin(ang)], axis=1).astype(np.float32)


def build(nc, x, mem, g_mix, w_in, conv_w, sinks, w_attn_o, w_conv_o, w_out, g_xattn, g_mem,
          w_xq, w_xkv, w_xo, g_ffn, w_gate_up, w_down, g_final, rope, out):
    with ExitStack() as ctx:
        def sem(name):
            return ctx.enter_context(nc.semaphore(name))

        KB = 1024
        base = -(-nc.sbuf_base // 32) * 32
        size = 200 * KB + 7552
        ctx.enter_context(nc.sbuf_tensor("arena", [P, size + base - nc.sbuf_base], mybir.dt.uint8))

        def at(name, off, shape, dt=F32):
            return nc.alloc_sbuf_tensor_at(name, shape, dt, offset=base + off)

        h_hi = at("h_hi", 0, [P, KT, SEQ], F32R)
        h_lo = at("h_lo", 32 * KB, [P, KT, SEQ], F32R)
        raw = at("raw", 64 * KB, [P, RAW, 2, 512])
        w_hi = at("w_hi", 80 * KB, [P, SPL, 512], F32R)
        w_lo = at("w_lo", 88 * KB, [P, SPL, 512], F32R)
        x_sq = at("x_sq", 96 * KB, [P, D])
        q_t = at("q_t", 96 * KB, [P, PAIRS, SEQ])
        k_t = at("k_t", 112 * KB, [P, NKV, SEQ])
        v_d = at("v_d", 120 * KB, [P, TT, NKV, 2, HD])
        acc = at("acc", 96 * KB, [P, KT, SEQ])
        mem_n = at("mem_n", 96 * KB, [P, MT, D])
        mem_sq = at("mem_sq", 112 * KB, [P, D])
        x_nat = at("x_nat", 128 * KB, [P, TT, D])
        conv_t = at("conv_t", 128 * KB, [P, CT, 2, SEQ], F32R)
        stage = at("stage", 160 * KB, [P, TT, 8, HD])
        kdup = at("kdup", 168 * KB, [P, TT, NKV, 2, HD])
        rtmp = at("rtmp", 176 * KB, [P, 4, 8, HALF])
        probs = at("probs", 144 * KB, [P, 3, 2, 256])
        vpad = at("vpad", 150 * KB, [P, 4, 2 + SEQ])
        attn_t = at("attn_t", 160 * KB, [P, PAIRS, 2, SEQ], F32R)
        mrg_t = at("mrg_t", 128 * KB, [P, KT, 2, SEQ], F32R)
        mem_t = at("mem_t", 128 * KB, [P, KT, 2, NMEM], F32R)
        xo_t = at("xo_t", 128 * KB, [P, XH, 2, SEQ], F32R)
        xq_t = at("xq_t", 160 * KB, [P, XH, SEQ])
        kx = at("kx", 168 * KB, [P, XH, NMEM])
        vx = at("vx", 172 * KB, [P, MT, XH * XHD])
        px = at("px", 176 * KB, [P, XH * TT, NMEM])
        act_t = at("act_t", 144 * KB, [P, 4, 2, SEQ], F32R)
        up = at("up", 160 * KB, [P, 4, SEQ])
        gfin = at("gfin", 176 * KB, [P, D])
        y_out = at("y_out", 0, [P, TT, D])
        tile4 = at("tile4", 192 * KB, [P, 4, SEQ])
        pt_x = at("pt_x", 192 * KB, [P, 2, MT, SEQ])
        o = 200 * KB
        rbc = at("rbc", o, [P, SEQ]); o += 2 * KB
        pt_s = at("pt_s", o, [P, 2, 2, P]); ssq = at("ssq", o, [P, SEQ]); o += 2 * KB
        mask = at("mask", o, [P, 256]); o += KB
        ident = at("ident", o, [P, P]); o += 512
        ones = at("ones", o, [P, P]); o += 512
        prow = at("prow", 192 * KB, [88, P])
        par = at("par", o, [P, 88]); o += 352
        cs = at("cs", o, [P, TT, 2, HALF]); o += 256
        snk = at("snk", o, [P, NQ]); nsnk = at("nsnk", o + 64, [P, NQ]); o += 128
        ssx = at("ssx", o, [P, TT])
        rcol = at("rcol", o + 32, [P, TT])
        rtm = at("rtm", o + 64, [P, TT])
        ssm = at("ssm", o + 96, [P, MT])
        rmem = at("rmem", o + 128, [P, MT])
        rtm2 = at("rtm2", o + 160, [P, MT])
        rtp = at("rtp", o + 192, [P, TT])
        o += 224
        st_a = at("st_a", o, [P, 4, 6, 2])
        o += 192
        st_x = at("st_x", o, [P, 4, XH * TT])
        o += 256
        gmix, gx, gm, gf = (par[:, KT * i:KT * i + KT] for i in range(4))
        assert o <= size, o

        bank = [ctx.enter_context(nc.psum_tensor(f"bank{i}", [P, 512], F32)) for i in range(8)]
        A, B = bank[0:4], bank[4:8]

        def banks(g):
            if g < G_MERGE:
                return B if g >= G_CONV or g == 1 else A
            return A if g % 2 else B

        s_x = [sem(f"x_loaded{t}") for t in range(TT)]
        s_prow = sem("gains_loaded")
        s_small = sem("rope_sinks_loaded")
        s_mem = sem("mem_loaded")
        s_gfin = sem("gfinal_loaded")
        s_const0 = sem("constants_cleared")
        s_const = sem("constants_ready")
        s_raw = [sem(f"raw_loaded{i}") for i in range(RAW)]
        s_hi = sem("weights_hi_ready")
        s_lo = sem("weights_lo_ready")
        s_used = sem("weights_used")
        s_done = sem("bank_done")
        s_freed = sem("bank_freed")
        s_parT = sem("gains_transposed")
        s_par = sem("gains_ready")
        s_xT = sem("x_transposed")
        s_xhi = sem("x_hi_ready")
        s_xlo = sem("x_lo_ready")
        s_ssx = sem("x_squares_ready")
        s_rcol = sem("x_rstd_ready")
        s_rT = sem("rstd_broadcast")
        s_rbc = sem("rbc_ready")
        s_stage = sem("qkv_stage_ready")
        s_tr = sem("qkv_transposed")
        s_qkv = sem("qkv_ready")
        s_s = sem("scores_done")
        s_sm = sem("masked_scores_ready")
        s_e = sem("exp_done")
        s_p = sem("probs_ready")
        s_pT = sem("probs_transposed")
        s_pts = sem("probs_t_ready")
        s_o = sem("heads_done")
        s_ohi = sem("heads_hi_ready")
        s_olo = sem("heads_lo_ready")
        s_chi = sem("conv_hi_ready")
        s_clo = sem("conv_lo_ready")
        s_gate = sem("gate_ready")
        s_mg = sem("merged_tiles")
        s_mhi = sem("merged_hi_ready")
        s_mlo = sem("merged_lo_ready")
        s_hs = sem("h_sum_ready")
        s_hhi = sem("h_hi_ready")
        s_hlo = sem("h_lo_ready")
        s_ssm = sem("mem_squares_ready")
        s_mn = sem("mem_normalised")
        s_mT = sem("mem_transposed")
        s_mthi = sem("mem_hi_ready")
        s_mtlo = sem("mem_lo_ready")
        s_xs = sem("xscores_done")
        s_xm = sem("xmax_ready")
        s_xe = sem("xexp_done")
        s_xp = sem("xprobs_ready")
        s_xpT = sem("xprobs_transposed")
        s_xpt = sem("xprobs_t_ready")
        s_xoo = sem("xheads_done")
        s_xohi = sem("xheads_hi_ready")
        s_xolo = sem("xheads_lo_ready")
        s_upp = sem("hidden_ready")
        s_ahi = sem("hidden_hi_ready")
        s_alo = sem("hidden_lo_ready")
        s_fsq = sem("final_squares_ready")
        s_fs = sem("final_sum_done")
        s_fr = sem("final_rstd_ready")
        s_fT = sem("final_transposed")
        s_y = sem("y_ready")
        s_out = sem("out_stored")
        s_var = sem("variance_ready")
        s_root = sem("root_ready")
        s_v = sem("vector_step")

        block = ctx.enter_context(nc.Block())

        @block.sync
        def _(sp):
            sp.dma_start(x_nat[:, 0, :], x[0, 0:P, :]).then_inc(s_x[0], 16)
            for i, g in enumerate((g_mix, g_xattn, g_mem, g_ffn)):
                sp.dma_start(prow[KT * i:KT * i + KT, :], g.rearrange("l (k p) -> (l k) p", p=P)).then_inc(s_prow, 16)
            sp.dma_start(prow[4 * KT:4 * KT + TAPS * CT, :],
                         conv_w.rearrange("l t (k p) -> (l t k) p", p=P)).then_inc(s_prow, 16)
            for t in range(1, TT):
                sp.dma_start(x_nat[:, t, :], x[0, t * P:(t + 1) * P, :]).then_inc(s_x[t], 16)

            def load(n0, per, i, c, w, row, col):
                n = n0 + c
                free = 2 * (n - RAW) + 2
                if i is None:
                    if n >= RAW:
                        sp.wait_ge(s_lo, free)
                    src = w[row:row + 256, col:col + 512].rearrange("(b p) n -> p b n", p=P)
                    sp.dma_start(raw[:, n % RAW, :, :], src).then_inc(s_raw[n % RAW], 16)
                else:
                    need = sp.to_reg(i * (2 * per) + free)
                    src = w[bass.ds(row, 256), bass.ds(col, 512)].rearrange("(b p) n -> p b n", p=P)
                    sp.dma_start(raw[:, n % RAW, :, :], src).wait_op(s_lo, need, "sem-ge").then_inc(s_raw[n % RAW], 16)

            wi, wc, wa, wo = w_in[0], w_conv_o[0], w_attn_o[0], w_out[0]
            for g, col in enumerate((Q0, Q0 + 512, K0)):
                for c in range(KT // 2):
                    load(B_QKV // 2 + 8 * g, 0, None, c, wi, 256 * c, col)
                    if g == 0 and c == RAW - 1:
                        sp.dma_start(cs[:, :, :, :].rearrange("p t a e -> p t (a e)"),
                                     rope.rearrange("(t p) e -> p t e", p=P)).then_inc(s_small, 16)
                        sp.dma_start(snk[:, :], sinks.partition_broadcast(P)[:, 0, :]).then_inc(s_small, 16)
            with sp.Fori(0, 2) as i:
                for g, col in enumerate((CC0, CH0, CB0)):
                    for c in range(KT // 2):
                        load(B_CONV // 2 + 8 * g, 24, i, c, wi, 256 * c, i * 512 + col)
            with sp.Fori(0, 4) as i:
                n = B_MERGE // 2
                for w, col, chunks in ((wi, GC0, 8), (wc, 0, 4), (wi, GA0, 8), (wa, 0, 4)):
                    for c in range(chunks):
                        load(n, MERGE_BLOCKS // 2, i, c, w, 256 * c, i * 512 + col)
                    n += chunks
            with sp.Fori(0, 4) as i:
                for c in range(8):
                    load(B_WOUT // 2, 8, i, c, wo, 256 * c, i * 512)
            for n, w, col in ((B_XQ, w_xq[0], 0), (B_XK, w_xkv[0], 0), (B_XV, w_xkv[0], 512)):
                for c in range(8):
                    load(n // 2, 0, None, c, w, 256 * c, col)
            for g in range(4):
                for c in range(2):
                    load(B_XO // 2 + 2 * g, 0, None, c, w_xo[0], 256 * c, 512 * g)
            wgu, wd = w_gate_up[0], w_down[0]
            for c in range(8):
                load(B_G0 // 2, 0, None, c, wgu, 256 * c, 0)
            for c in range(8):
                load(B_U0 // 2, 0, None, c, wgu, 256 * c, FF)
            with sp.Fori(0, FG - 1) as i:
                for c in range(8):
                    load(B_FFN // 2, 24, i, c, wgu, 256 * c, i * 512 + 512)
                for g in range(4):
                    for c in range(2):
                        load(B_FFN // 2 + 8 + 2 * g, 24, i, c, wd, i * 512 + 256 * c, 512 * g)
                for c in range(8):
                    load(B_FFN // 2 + 16, 24, i, c, wgu, 256 * c, i * 512 + FF + 512)
            for g in range(4):
                for c in range(2):
                    load(B_LAST // 2 + 2 * g, 0, None, c, wd, (FG - 1) * 512 + 256 * c, 512 * g)
            for t in range(TT):
                sp.wait_ge(s_y, 4 * (t + 1))
                sp.dma_start(out[0, t * P:(t + 1) * P, :], y_out[:, t, :]).then_inc(s_out, 16)
            sp.wait_ge(s_out, 16 * TT)

        @block.gpsimd
        def _(pool):
            pool.memset(ident[:, :], 0.0).then_inc(s_const0, 1)
            pool.memset(mask[:, :], 0.0).then_inc(s_const0, 1)
            pool.memset(ones[:, :], 1.0).then_inc(s_const, 1)
            pool.wait_ge(s_const0, 2)
            pool.affine_select(out=ident[:, :], in_=ident[:, :], compare_op=ALU.not_equal, fill=1.0,
                               base=0, pattern=[[-1, P]], channel_multiplier=1).then_inc(s_const, 1)
            pool.affine_select(out=mask[:, :], in_=mask[:, :], compare_op=ALU.is_gt, fill=NEG,
                               base=0, pattern=[[1, 256]], channel_multiplier=-1).then_inc(s_const0, 1)
            pool.wait_ge(s_const0, 3)
            pool.affine_select(out=mask[:, :], in_=mask[:, :], compare_op=ALU.is_ge, fill=NEG,
                               base=P, pattern=[[-1, 256]], channel_multiplier=1).then_inc(s_const, 1)
            pool.wait_ge(s_mlo, KT)
            pool.dma_start(mem_n[:, :, :], mem[0].rearrange("(t p) n -> p t n", p=P)).then_inc(s_mem, 16)
            pool.wait_ge(s_done, 4 * G_G0 + 1)
            pool.dma_start(gfin[:, :], g_final.partition_broadcast(P)).then_inc(s_gfin, 16)

        @block.tensor
        def _(pe):
            def wait_block(b0, per, i, k):
                pe.wait_ge(s_lo, b0 + k + 1 + (i * per if i is not None else 0))

            def columns(bk, k, n, hi, lo, width=SEQ, wait_bank=None):
                s = k % SPL
                for j in range(4):
                    if k == 0 and wait_bank:
                        wait_bank(j)
                    c = slice(j * P, (j + 1) * P)
                    o_ = bk[j][:, 0:width]
                    pe.matmul(o_, w_hi[:, s, c], hi, start=(k == 0), stop=False)
                    pe.matmul(o_, w_hi[:, s, c], lo, start=False, stop=False)
                    mm = pe.matmul(o_, w_lo[:, s, c], hi, start=False, stop=(k == n - 1))
                    if k == n - 1:
                        mm.then_inc(s_done, 1)
                if k < n - 1:
                    mm.then_inc(s_used, 1)

            def rows(bk, k, n, hi, lo, tiles, inc, wait_bank=None):
                s = k % SPL
                for j in range(tiles):
                    if k == 0 and wait_bank:
                        wait_bank(j)
                    c = slice(j * P, (j + 1) * P)
                    pe.matmul(bk[j][:, :], hi[:, c], w_hi[:, s, :], start=(k == 0), stop=False)
                    pe.matmul(bk[j][:, :], hi[:, c], w_lo[:, s, :], start=False, stop=False)
                    mm = pe.matmul(bk[j][:, :], lo[:, c], w_hi[:, s, :], start=False, stop=(k == n - 1))
                    if k == n - 1:
                        mm.then_inc(s_done, inc)
                if k < n - 1:
                    mm.then_inc(s_used, 1)

            def freed(g, per=0, i=None):
                return lambda j: pe.wait_ge(s_freed, 4 * (g - 2) + j + 1 + (i * per if i is not None else 0))

            pe.wait_ge(s_const, 3)
            for m in range(TT * 4):
                t, kg = divmod(m, 4)
                if kg == 0:
                    pe.wait_ge(s_x[t], 16)
                if m >= 8:
                    pe.wait_ge(s_xlo, m - 7)
                for q in range(4):
                    k = 4 * kg + q
                    mm = pe.transpose(bank[m % 8][:, q * P:(q + 1) * P], x_nat[:, t, k * P:(k + 1) * P], ident[:, :])
                mm.then_inc(s_xT, 1)
                if m == 3:
                    pe.wait_ge(s_prow, 80)
                    pe.transpose(bank[7][:, 0:88], prow[:, :], ident[0:88, 0:88]).then_inc(s_parT, 1)
                if m == 6:
                    pe.wait_ge(s_par, 1)

            def qkv_transposes(g, t):
                pe.wait_ge(s_stage, 4 * g + t + 1)
                src = stage[:, t, :, :].rearrange("p h d -> p (h d)") if g < 2 else kdup[:, t, :, :, :].rearrange("p h a d -> p (h a d)")
                for q in range(4):
                    mm = pe.transpose(banks(g)[t][:, q * P:(q + 1) * P], src[:, q * P:(q + 1) * P], ident[:, :])
                mm.then_inc(s_tr, 1)

            for g in range(3):
                for k in range(KT):
                    wait_block(B_QKV + KT * g, 0, None, k)
                    if g == 0 and k == 0:
                        pe.wait_ge(s_xlo, 16)
                    if g == 1 and k == 0:
                        pe.wait_ge(s_rbc, 1)
                    if g == 2 and k == 0:
                        pe.wait_ge(s_qkv, 4)
                    rows(banks(g), k, KT, h_hi[:, k, :], h_lo[:, k, :], TT, 1)
                    if g == 0 and k == 13:
                        pe.wait_ge(s_rcol, 1)
                        for t in range(TT):
                            mm = pe.matmul(B[0][:, t * P:(t + 1) * P], rcol[:, t:t + 1].to_broadcast([P, P]), ident[:, :],
                                           start=True, stop=True)
                        mm.then_inc(s_rT, 1)
                    if g and 6 <= k < 10:
                        qkv_transposes(g - 1, k - 6)

            S0, S1, PT, O = A

            def scores(u):
                p, n = divmod(u, TT)
                c0 = 0 if n else P
                pe.wait_ge(s_qkv, 12)
                if u:
                    pe.wait_ge(s_sm, u)
                for e in range(2):
                    r = slice(HD * e, HD * e + HD)
                    mm = pe.matmul((S0, S1)[e][:, c0:256], q_t[r, p, n * P:(n + 1) * P],
                                   k_t[r, p // 2, (n - 1) * P + c0:(n + 1) * P], start=True, stop=True)
                mm.then_inc(s_s, 1)

            def probs_transposes(u):
                n = u % TT
                pe.wait_ge(s_p, u + 1)
                if u:
                    pe.wait_ge(s_pts, u)
                else:
                    pe.wait_ge(s_qkv, 12)
                for c in range(0 if n else 1, 2):
                    for e in range(2):
                        mm = pe.transpose(PT[:, (2 * c + e) * P:(2 * c + e + 1) * P],
                                          probs[:, u % 3, e, c * P:(c + 1) * P], ident[:, :])
                mm.then_inc(s_pT, 1)

            def heads(u):
                p, n = divmod(u, TT)
                pe.wait_ge(s_pts, u + 1)
                if u:
                    pe.wait_ge(s_olo, u)
                for c in range(0 if n else 1, 2):
                    mm = pe.matmul(O[:, 0:256], v_d[:, n - 1 + c, p // 2, :, :].rearrange("p a d -> p (a d)"),
                                   pt_s[:, c, :, :].rearrange("p e q -> p (e q)"), start=(c == 0 or n == 0), stop=(c == 1))
                mm.then_inc(s_o, 1)

            for g in range(6):
                for k in range(KT):
                    wait_block(B_CONV + KT * g, 0, None, k)
                    if g == 0 and k == 0:
                        pe.wait_ge(s_qkv, 8)

                    def wb(j):
                        if g:
                            pe.wait_ge(s_freed, 4 * (G_CONV + g - 1) + j + 1)
                    columns(B, k, KT, h_hi[:, k, :], h_lo[:, k, :], wait_bank=wb)
                    if g == 0 and 6 <= k < 10:
                        qkv_transposes(2, k - 6)
                    slot = KT // 2 * g + k // 2
                    if k % 2 == 0:
                        if 0 <= slot - 11 < UNITS:
                            heads(slot - 11)
                    else:
                        if 0 <= slot - 7 < UNITS:
                            scores(slot - 7)
                        if 0 <= slot - 9 < UNITS:
                            probs_transposes(slot - 9)

            pe.wait_ge(s_olo, UNITS)
            with pe.Fori(0, 4) as i:
                b, g = B_MERGE, G_MERGE
                for kind in range(4):
                    n = KT if kind % 2 == 0 else CT
                    for k in range(n):
                        wait_block(b, MERGE_BLOCKS, i, k)
                        if kind % 2 == 0:
                            hi, lo = h_hi[:, k, :], h_lo[:, k, :]
                        else:
                            if kind == 1:
                                pe.wait_ge(s_clo, k + 1)
                            src = conv_t if kind == 1 else attn_t
                            hi, lo = src[:, k, 0, :], src[:, k, 1, :]
                        columns(banks(g), k, n, hi, lo, wait_bank=freed(g, 16, i))
                    b += n
                    g += 1
            with pe.Fori(0, 2) as i:
                for c in range(2):
                    for k in range(KT):
                        wait_block(B_WOUT + KT * c, 2 * KT, i, k)
                        pe.wait_ge(s_mlo, k + 1)
                        columns(banks(G_WOUT + c), k, KT, mrg_t[:, k, 0, :], mrg_t[:, k, 1, :],
                                wait_bank=freed(G_WOUT + c, 8, i))
            for k in range(KT):
                wait_block(B_XQ, 0, None, k)
                pe.wait_ge(s_hlo, k + 1)
                columns(banks(G_XQ), k, KT, h_hi[:, k, :], h_lo[:, k, :], wait_bank=freed(G_XQ))
                if k == 8:
                    pe.wait_ge(s_hs, 2 * KT)
                    pe.matmul(B[0][:, :], ones[:, :], ssq[:, :], start=True, stop=True).then_inc(s_rT, 1)
                    pe.wait_ge(s_mn, MT)
                if 9 <= k < 13:
                    for m in range(2 * (k - 9), 2 * (k - 9) + 2):
                        t, kg = divmod(m, 4)
                        if m == 0:
                            pe.wait_ge(s_rbc, 2)
                        if m >= 4:
                            pe.wait_ge(s_mtlo, m - 3)
                        for q in range(4):
                            mm = pe.transpose(B[m % 4][:, q * P:(q + 1) * P],
                                              mem_n[:, t, (4 * kg + q) * P:(4 * kg + q + 1) * P], ident[:, :])
                        mm.then_inc(s_mT, 1)
            for k in range(KT):
                wait_block(B_XK, 0, None, k)
                if k == 0:
                    pe.wait_ge(s_mtlo, 8)
                columns(banks(G_XK), k, KT, mem_t[:, k, 0, :], mem_t[:, k, 1, :], width=NMEM)

            XU = XH * TT
            for k in range(KT):
                wait_block(B_XV, 0, None, k)
                rows(banks(G_XV), k, KT, mem_t[:, k, 0, :], mem_t[:, k, 1, :], MT, 2, wait_bank=freed(G_XV))
                h, t = divmod(k, TT)
                if k == 0:
                    pe.wait_ge(s_freed, 4 * G_XK + 4)
                if k >= 2:
                    pe.wait_ge(s_xe, k - 1)
                pe.matmul(B[k % 2][:, 0:NMEM], xq_t[:, h, t * P:(t + 1) * P], kx[:, h, :],
                          start=True, stop=True).then_inc(s_xs, 1)

            def x_transposes(h):
                for c in range(MT):
                    if h:
                        pe.wait_ge(s_xpt, 2 * (h - 1) + c + 1)
                    for t in range(TT):
                        pe.wait_ge(s_xp, TT * h + t + 1)
                        mm = pe.transpose(B[2 + c][:, t * P:(t + 1) * P], px[:, TT * h + t, c * P:(c + 1) * P], ident[:, :])
                    mm.then_inc(s_xpT, 1)

            def x_heads(h):
                if h == 0:
                    pe.wait_ge(s_freed, 4 * G_XV + 4)
                pe.wait_ge(s_xpt, 2 * h + 2)
                if h >= 2:
                    pe.wait_ge(s_xolo, h - 1)
                for c in range(MT):
                    mm = pe.matmul(A[2 + h % 2][:, :], vx[:, c, h * XHD:(h + 1) * XHD], pt_x[:, h % 2, c, :],
                                   start=(c == 0), stop=(c == MT - 1))
                mm.then_inc(s_xoo, 1)

            x_transposes(0)
            for h in range(1, XH):
                x_transposes(h)
                x_heads(h - 1)
            x_heads(XH - 1)
            for c in range(4):
                for k in range(XH):
                    wait_block(B_XO + XH * c, 0, None, k)
                    pe.wait_ge(s_xolo, k + 1)

                    def wb(j):
                        if c < 2:
                            pe.wait_ge(s_xolo, XH)
                        if c:
                            pe.wait_ge(s_freed, 4 * (G_XO + c - 2) + j + 1)
                    columns(banks(G_XO + c), k, XH, xo_t[:, k, 0, :], xo_t[:, k, 1, :], wait_bank=wb)

            def hidden(g, b, per_g, per_b, i, norm=False):
                for k in range(KT):
                    wait_block(b, per_b, i, k)
                    if norm:
                        pe.wait_ge(s_hlo, KT + k + 1)
                    columns(banks(g), k, KT, h_hi[:, k, :], h_lo[:, k, :], wait_bank=freed(g, per_g, i))
                    if norm and k == 8:
                        pe.wait_ge(s_hs, 4 * KT)
                        pe.matmul(A[0][:, :], ones[:, :], ssq[:, :], start=True, stop=True).then_inc(s_rT, 1)

            def down(g, b, alo, per_g, per_b, i):
                for c in range(4):
                    for k in range(4):
                        wait_block(b + 4 * c, per_b, i, k)
                        if c == 0:
                            pe.wait_ge(s_alo, alo + k + 1 + (i * 4 if i is not None else 0))
                        columns(banks(g + c), k, 4, act_t[:, k, 0, :], act_t[:, k, 1, :], wait_bank=freed(g + c, per_g, i))

            hidden(G_G0, B_G0, 0, 0, None, norm=True)
            pe.wait_ge(s_rbc, 3)
            hidden(G_U0, B_U0, 0, 0, None)
            with pe.Fori(0, FG - 1) as i:
                hidden(G_FFN, B_FFN, 24, FFN_BLOCKS, i)
                down(G_FFN + 1, B_FFN + KT, 0, 24, FFN_BLOCKS, i)
                hidden(G_FFN + 5, B_FFN + 2 * KT, 24, FFN_BLOCKS, i)
            down(G_LAST, B_LAST, 4 * (FG - 1), 0, 0, None)

            FB = banks(G_LAST)
            pe.wait_ge(s_fsq, KT)
            for t in range(TT):
                mm = pe.matmul(FB[0][:, t:t + 1], ssq[:, t * P:(t + 1) * P], ones[:, 0:1], start=True, stop=True)
            mm.then_inc(s_fs, 1)
            for m in range(TT * 4):
                t, kg = divmod(m, 4)
                bk = bank[(m + 1) % 8] if FB is A else bank[(m + 5) % 8]
                if m >= 7:
                    pe.wait_ge(s_y, m - 7 if m > 7 else 1)
                if m == 7:
                    pe.wait_ge(s_fr, 1)
                if m >= 8:
                    pe.wait_ge(s_y, m - 7)
                for q in range(4):
                    mm = pe.transpose(bk[:, q * P:(q + 1) * P], acc[:, 4 * kg + q, t * P:(t + 1) * P], ident[:, :])
                mm.then_inc(s_fT, 1)

        @block.scalar
        def _(act):
            def hi(b0, g, k, gain=None, per=0, gper=0, i=None):
                n = (b0 + k) // 2
                s = (b0 + k) % SPL
                if k % 2 == 0:
                    act.wait_ge(s_raw[n % RAW], 16 * (n // RAW + 1) + (i * (2 * per) if i is not None else 0))
                if k == SPL - 1 and g:
                    act.wait_ge(s_done, 4 * g + (i * (4 * gper) if i is not None else 0))
                elif b0 + k >= SPL:
                    before = g if k >= SPL else g - 1
                    act.wait_ge(s_used, b0 + k - SPL + 1 - before + (i * (per - gper) if i is not None else 0))
                sc = 1.0 if gain is None else gain[:, k:k + 1]
                nc.scalar.activation(w_hi[:, s, :], raw[:, n % RAW, (b0 + k) % 2, :], ACT.Copy, scale=sc).then_inc(s_hi, 1)

            def group(b0, g, n, gain=None, per=0, gper=0, i=None, after=None):
                for k in range(n):
                    hi(b0, g, k, gain, per, gper, i)
                    if after and n > 4 and 4 <= k < 8:
                        after(k - 4)
                if after and n <= 4:
                    for j in range(4):
                        after(j)

            for m in range(TT * 4):
                t, kg = divmod(m, 4)
                act.wait_ge(s_xT, m + 1)
                nc.scalar.activation(h_hi[:, 4 * kg:4 * kg + 4, t * P:(t + 1) * P],
                                     bank[m % 8][:, :].rearrange("p (k q) -> p k q", k=4), ACT.Copy).then_inc(s_xhi, 1)
                if m == 4:
                    act.wait_ge(s_parT, 1)
                    nc.scalar.activation(par[:, :], bank[7][:, 0:88], ACT.Copy).then_inc(s_par, 1)
                    act.wait_ge(s_par, 1)

            def root(n, dst, var):
                act.wait_ge(s_var, n)
                nc.scalar.activation(dst, var, ACT.Sqrt).then_inc(s_root, 1)

            def q_out(g, t):
                act.wait_ge(s_tr, 4 * g + t + 1)
                dst = q_t[:, 4 * g:4 * g + 4, t * P:(t + 1) * P] if g < 2 else k_t[:, :, t * P:(t + 1) * P]
                nc.scalar.activation(dst, banks(g)[t][:, :].rearrange("p (k q) -> p k q", k=4), ACT.Copy).then_inc(s_qkv, 1)

            for g in range(3):
                for k in range(KT):
                    hi(B_QKV + KT * g, G_QKV + g, k, gmix)
                    if g == 0 and 4 <= k < 8:
                        if k > 4:
                            act.wait_ge(s_ssx, k - 4)
                        nc.scalar.activation(x_sq[:, :], x_nat[:, k - 4, :], ACT.Square,
                                             accum_out=ssx[:, k - 4:k - 3]).then_inc(s_ssx, 1)
                    if g == 0 and k == 10:
                        root(1, rcol[:, :], rtm[:, :])
                    if g and 10 <= k < 14:
                        q_out(g - 1, k - 10)

            def exps(u):
                r, n = u % 3, u % TT
                s, c0 = st_a[:, u % 4], 0 if n else P
                act.wait_ge(s_sm, u + 1)
                for e in range(2):
                    nc.scalar.activation(probs[:, r, e, c0:256], probs[:, r, e, c0:256], ACT.Exp, bias=s[:, 1, e:e + 1],
                                         accum_out=s[:, 2, e:e + 1])
                nc.scalar.activation(s[:, 3, :], s[:, 4, :], ACT.Exp).then_inc(s_e, 1)

            def probs_out(u):
                act.wait_ge(s_pT, u + 1)
                if u:
                    act.wait_ge(s_o, u)
                c0 = 0 if u % TT else 1
                nc.scalar.activation(pt_s[:, c0:2, :, :].rearrange("p c e q -> p (c e q)"),
                                     PT_[:, 256 * c0:512], ACT.Copy).then_inc(s_pts, 1)

            def heads_hi(u):
                p, n = divmod(u, TT)
                act.wait_ge(s_o, u + 1)
                for e in range(2):
                    r = slice(HD * e, HD * e + HD)
                    last = nc.scalar.activation(attn_t[r, p, 0, n * P:(n + 1) * P], O_[r, e * P:(e + 1) * P], ACT.Copy)
                last.then_inc(s_ohi, 1)

            PT_, O_ = A[2], A[3]
            for g in range(6):
                for k in range(KT):
                    hi(B_CONV + KT * g, G_CONV + g, k, gmix)
                    if g == 0 and 10 <= k < 14:
                        q_out(2, k - 10)
                    if g == 3 and 8 <= k < 12:
                        act.wait_ge(s_freed, 4 * (G_CONV + 2) + k - 7)
                        nc.scalar.activation(conv_t[:, k - 8, 0, :], tile4[:, k - 8, :], ACT.Copy).then_inc(s_chi, 1)
                    if k % 2:
                        slot = KT // 2 * g + k // 2
                        if 0 <= slot - 12 < UNITS:
                            heads_hi(slot - 12)
                        if 0 <= slot - 11 < UNITS:
                            probs_out(slot - 11)
                        if 0 <= slot - 8 < UNITS:
                            exps(slot - 8)

            def conv_hi(j):
                act.wait_ge(s_freed, 4 * (G_CONV + 5) + j + 1)
                nc.scalar.activation(conv_t[:, 4 + j, 0, :], tile4[:, j, :], ACT.Copy).then_inc(s_chi, 1)

            def gate(g, func, gper=0, i=None):
                def f(j):
                    act.wait_ge(s_freed, 4 * g + j + 1 + (i * (4 * gper) if i is not None else 0))
                    nc.scalar.activation(tile4[:, j, :], tile4[:, j, :], func).then_inc(s_gate, 1)
                return f

            def merged_hi(k):
                if k == 0:
                    act.wait_ge(s_done, 4 * (G_MERGE + 13) + 4)
                if k == 8:
                    act.wait_ge(s_done, 4 * (G_MERGE + 15) + 4)
                if k >= 8:
                    act.wait_ge(s_mg, k + 1)
                nc.scalar.activation(mrg_t[:, k, 0, :], acc[:, k, :], ACT.Copy).then_inc(s_mhi, 1)

            M, G, MB = B_MERGE, G_MERGE, MERGE_BLOCKS
            group(M, G, KT, gmix, after=conv_hi)
            with act.Fori(0, 3) as i:
                group(M + KT, G + 1, CT, None, MB, 4, i, gate(G, ACT.Sigmoid, 4, i))
                group(M + KT + CT, G + 2, KT, gmix, MB, 4, i)
                group(M + 2 * KT + CT, G + 3, CT, None, MB, 4, i, gate(G + 2, ACT.Sigmoid, 4, i))
                group(M + MB, G + 4, KT, gmix, MB, 4, i)
            M += 3 * MB
            G += 12
            group(M + KT, G + 1, CT, after=gate(G, ACT.Sigmoid))
            act.wait_ge(s_mg, 8)
            for k in range(KT):
                hi(M + KT + CT, G + 2, k, gmix)
                if k >= 8:
                    merged_hi(k - 8)
            group(M + 2 * KT + CT, G + 3, CT, after=gate(G + 2, ACT.Sigmoid))

            def h_hi_sq(t, j, src, sq):
                act.wait_ge(s_hs, 2 * t + 1)
                nc.scalar.activation(h_hi[:, t % KT, :], src, ACT.Copy)
                nc.scalar.activation(sq, src, ACT.Square).then_inc(s_hhi, 1)

            for k in range(KT):
                hi(B_WOUT, G_WOUT, k)
                if k >= 6 and k < 14:
                    merged_hi(k + 2)
            for c in range(1, 4):
                group(B_WOUT + KT * c, G_WOUT + c, KT, after=lambda j: h_hi_sq(4 * (c - 1) + j, j, tile4[:, j, :], acc[:, 12 + j, :]))
                if c == 2:
                    for t in range(MT):
                        if t:
                            act.wait_ge(s_ssm, t)
                        else:
                            act.wait_ge(s_mem, 16)
                        nc.scalar.activation(mem_sq[:, :], mem_n[:, t, :], ACT.Square, accum_out=ssm[:, t:t + 1]).then_inc(s_ssm, 1)
            root(2, rmem[:, :], rtm2[:, :])
            for k in range(KT):
                hi(B_XQ, G_XQ, k, gx)
                if 4 <= k < 8:
                    h_hi_sq(12 + k - 4, k - 4, tile4[:, k - 4, :], acc[:, 12 + k - 4, :])
                if k == 12:
                    root(3, rbc[:, :], acc[:, 8, :])
                if 12 <= k < 16:
                    for m in range(2 * (k - 12), 2 * (k - 12) + 2):
                        t, kg = divmod(m, 4)
                        act.wait_ge(s_mT, m + 1)
                        nc.scalar.activation(mem_t[:, 4 * kg:4 * kg + 4, 0, t * P:(t + 1) * P],
                                             B[m % 4][:, :].rearrange("p (k q) -> p k q", k=4), ACT.Copy).then_inc(s_mthi, 1)
            group(B_XK, G_XK, KT, gm)

            def x_exp(u):
                act.wait_ge(s_xm, u + 1)
                nc.scalar.activation(px[:, u, :], B[u % 2][:, 0:NMEM], ACT.Exp, bias=st_x[:, 1, u:u + 1],
                                     scale=XHD ** -0.5, accum_out=st_x[:, 2, u:u + 1]).then_inc(s_xe, 1)

            for k in range(KT):
                hi(B_XV, G_XV, k, gm)
                if k >= 4:
                    x_exp(k - 4)
            for u in range(12, 16):
                x_exp(u)
            for k in range(XH):
                hi(B_XO, G_XO, k)

            def x_hi(h):
                act.wait_ge(s_xoo, h + 1)
                nc.scalar.activation(xo_t[:, h, 0, :], A[2 + h % 2][:, :], ACT.Copy).then_inc(s_xohi, 1)

            for h in range(XH):
                for c in range(MT):
                    act.wait_ge(s_xpT, 2 * h + c + 1)
                    if h >= 2:
                        act.wait_ge(s_xoo, h - 1)
                    nc.scalar.activation(pt_x[:, h % 2, c, :], B[2 + c][:, :], ACT.Copy).then_inc(s_xpt, 1)
                if h:
                    x_hi(h - 1)
            x_hi(XH - 1)

            def xo_after(c):
                return lambda j: h_hi_sq(KT + 4 * c + j, j, acc[:, 4 * c + j, :], tile4[:, j, :])

            for c in range(1, 4):
                group(B_XO + XH * c, G_XO + c, XH, after=xo_after(c - 1))
            for k in range(KT):
                hi(B_G0, G_G0, k, gf)
                if 4 <= k < 8:
                    xo_after(3)(k - 4)
                if k == 12:
                    root(4, rbc[:, :], up[:, 0, :])

            def hidden_hi(n0, i=None):
                def f(j):
                    act.wait_ge(s_upp, n0 + j + 1 + (i * 4 if i is not None else 0))
                    nc.scalar.activation(act_t[:, j, 0, :], tile4[:, j, :], ACT.Copy).then_inc(s_ahi, 1)
                return f

            group(B_U0, G_U0, KT, gf, after=gate(G_G0, ACT.Silu))
            with act.Fori(0, FG - 1) as i:
                b, g, per = B_FFN, G_FFN, FFN_BLOCKS
                group(b, g, KT, gf, per, 6, i, hidden_hi(0, i))
                group(b + KT, g + 1, 4, None, per, 6, i, gate(g, ACT.Silu, 6, i))
                for c in range(1, 4):
                    group(b + KT + 4 * c, g + 1 + c, 4, None, per, 6, i)
                group(b + 2 * KT, g + 5, KT, gf, per, 6, i)
            group(B_LAST, G_LAST, 4, after=hidden_hi(4 * (FG - 1)))

            def f_sq(c):
                def f(j):
                    act.wait_ge(s_freed, 4 * (G_LAST + c) + j + 1)
                    nc.scalar.activation(tile4[:, j, :], acc[:, 4 * c + j, :], ACT.Square).then_inc(s_hhi, 1)
                return f

            for c in range(1, 4):
                group(B_LAST + 4 * c, G_LAST + c, 4, after=f_sq(c - 1))
            for j in range(4):
                f_sq(3)(j)
            root(5, rcol[:, :], rtm[:, :])

        @block.vector
        def _(dve):
            step = [0]

            def link(ins):
                ins.then_inc(s_v, 1)
                step[0] += 1
                dve.wait_ge(s_v, step[0])

            def rsqrt(n, dst, var, tmp, total):
                nc.vector.tensor_scalar(var, total, 1.0 / D, EPS, ALU.mult, ALU.add).then_inc(s_var, 1)
                dve.wait_ge(s_root, n)
                link(nc.vector.reciprocal(dst, dst))
                link(nc.vector.tensor_tensor(tmp, dst, dst, ALU.mult))
                link(nc.vector.tensor_tensor(tmp, tmp, var, ALU.mult))
                link(nc.vector.tensor_scalar(tmp, tmp, -0.5, 1.5, ALU.mult, ALU.add))
                return nc.vector.tensor_tensor(dst, dst, tmp, ALU.mult)

            def lo(b0, per, i, k, g=None):
                n = (b0 + k) // 2
                s = (b0 + k) % SPL
                dve.wait_ge(s_hi, b0 + k + 1 + (i * per if i is not None else 0))
                src = raw[:, n % RAW, (b0 + k) % 2, :]
                if g is None:
                    nc.vector.tensor_tensor(w_lo[:, s, :], src, w_hi[:, s, :], ALU.subtract).then_inc(s_lo, 1)
                else:
                    nc.vector.scalar_tensor_tensor(w_lo[:, s, :], src, g[:, k:k + 1], w_hi[:, s, :],
                                                   ALU.mult, ALU.subtract).then_inc(s_lo, 1)

            def group(b0, n, g=None, per=0, i=None, after=None):
                for k in range(n):
                    lo(b0, per, i, k, g)
                    if after and n > 4 and 3 <= k < 7:
                        after(k - 3)
                if after and n <= 4:
                    for j in range(4):
                        after(j)

            def out_of(g, j, per=0, i=None):
                dve.wait_ge(s_freed, 4 * g + j + 1 + (i * per if i is not None else 0))

            def done(g, j, per=0, i=None):
                dve.wait_ge(s_done, 4 * g + j + 1 + (i * per if i is not None else 0))

            for m in range(TT * 4):
                t, kg = divmod(m, 4)
                dve.wait_ge(s_xhi, m + 1)
                sl = (slice(None), slice(4 * kg, 4 * kg + 4), slice(t * P, (t + 1) * P))
                nc.vector.tensor_tensor(h_lo[sl], bank[m % 8][:, :].rearrange("p (k q) -> p k q", k=4), h_hi[sl],
                                        ALU.subtract).then_inc(s_xlo, 1)

            def rotate(v, nh, t):
                t1, t2 = v[:, :, 0:HALF], v[:, :, HALF:ROT]
                cos = cs[:, t, 0, :].unsqueeze(1).to_broadcast([P, nh, HALF])
                sin = cs[:, t, 1, :].unsqueeze(1).to_broadcast([P, nh, HALF])
                r = rtmp
                nc.vector.tensor_tensor(r[:, 0, 0:nh, :], t1, cos, ALU.mult)
                nc.vector.tensor_tensor(r[:, 1, 0:nh, :], t2, sin, ALU.mult)
                nc.vector.tensor_tensor(r[:, 2, 0:nh, :], t2, cos, ALU.mult)
                link(nc.vector.tensor_tensor(r[:, 3, 0:nh, :], t1, sin, ALU.mult))
                nc.vector.tensor_tensor(t1, r[:, 0, 0:nh, :], r[:, 1, 0:nh, :], ALU.subtract)
                return nc.vector.tensor_tensor(t2, r[:, 2, 0:nh, :], r[:, 3, 0:nh, :], ALU.add)

            def qkv_out(g, t):
                done(g, t)
                if g:
                    dve.wait_ge(s_tr, 4 * (g - 1) + t + 1)
                ps = banks(g)[t]
                nc.vector.tensor_scalar(stage[:, t, :, :].rearrange("p h d -> p (h d)"), ps[:, :], rcol[:, t:t + 1],
                                        None, ALU.mult).then_inc(s_freed, 1)
                out_of(g, t)
                if g < 2:
                    rotate(stage[:, t, :, :], 8, t).then_inc(s_stage, 1)
                else:
                    link(rotate(stage[:, t, 0:NKV, :], NKV, t))
                    for a in range(2):
                        nc.vector.tensor_copy(v_d[:, t, :, a, :], stage[:, t, NKV:2 * NKV, :])
                        last = nc.vector.tensor_copy(kdup[:, t, :, a, :], stage[:, t, 0:NKV, :])
                    last.then_inc(s_stage, 1)

            for k in range(KT):
                lo(B_QKV, 0, None, k, gmix)
                if k == 9:
                    dve.wait_ge(s_ssx, TT)
                    rsqrt(1, rcol[:, :], rtm[:, :], rtp[:, :], ssx[:, :]).then_inc(s_rcol, 1)
                    dve.wait_ge(s_rcol, 1)
                    dve.wait_ge(s_small, 32)
                    link(nc.vector.tensor_scalar(nsnk[:, :], snk[:, :], -1.0, None, ALU.mult))
            dve.wait_ge(s_rT, 1)
            nc.vector.tensor_copy(rbc[:, :], B[0][:, :]).then_inc(s_rbc, 1)
            group(B_QKV + KT, KT, gmix, after=lambda j: qkv_out(0, j))
            group(B_QKV + 2 * KT, KT, gmix, after=lambda j: qkv_out(1, j))

            def masked(u):
                p, n = divmod(u, TT)
                s, c0 = st_a[:, u % 4], 0 if n else P
                dve.wait_ge(s_s, u + 1)
                if u >= 3:
                    dve.wait_ge(s_pT, u - 2)
                for e in range(2):
                    ins = nc.vector.tensor_tensor_reduce(out=probs[:, u % 3, e, c0:256], in0=A[e][:, c0:256], in1=mask[:, c0:256],
                                                         scale=HD ** -0.5, scalar=NEG, op0=ALU.add, op1=ALU.max,
                                                         accum_out=s[:, 0, e:e + 1])
                link(ins)
                link(nc.vector.scalar_tensor_tensor(s[:, 1, :], s[:, 0, :], -1.0, nsnk[:, 2 * p:2 * p + 2], ALU.mult, ALU.min))
                nc.vector.tensor_tensor(s[:, 4, :], s[:, 1, :], snk[:, 2 * p:2 * p + 2], ALU.add).then_inc(s_sm, 1)

            def normalised(u):
                s, c0 = st_a[:, u % 4], 0 if u % TT else P
                dve.wait_ge(s_e, u + 1)
                link(nc.vector.tensor_tensor(s[:, 5, :], s[:, 2, :], s[:, 3, :], ALU.add))
                link(nc.vector.reciprocal(s[:, 5, :], s[:, 5, :]))
                for e in range(2):
                    ins = nc.vector.tensor_scalar(probs[:, u % 3, e, c0:256], probs[:, u % 3, e, c0:256], s[:, 5, e:e + 1], None, ALU.mult)
                ins.then_inc(s_p, 1)

            def heads_lo(u):
                p, n = divmod(u, TT)
                dve.wait_ge(s_ohi, u + 1)
                for e in range(2):
                    r = slice(HD * e, HD * e + HD)
                    q = slice(n * P, (n + 1) * P)
                    ins = nc.vector.tensor_tensor(attn_t[r, p, 1, q], A[3][r, e * P:(e + 1) * P], attn_t[r, p, 0, q], ALU.subtract)
                ins.then_inc(s_olo, 1)

            def c_out(g, j):
                done(G_CONV + g, j)
                nc.vector.tensor_tensor(tile4[:, j, :], B[j][:, :], rbc[:, :], ALU.mult).then_inc(s_freed, 1)

            def c_more(g, j):
                dve.wait_ge(s_freed, 4 * (G_CONV + g) + j + 1)
                link(nc.vector.tensor_tensor(tile4[:, j, :], tile4[:, j, :], rbc[:, :], ALU.mult))

            def v_out(g, j):
                done(G_CONV + g, j)
                nc.vector.tensor_tensor(vpad[:, j, 2:2 + SEQ], B[j][:, :], tile4[:, j, :], ALU.mult).then_inc(s_freed, 1)

            def v_more(g, j):
                ct = 4 * (g // 3) + j
                tap = [par[:, 4 * KT + CT * a + ct:4 * KT + CT * a + ct + 1] for a in range(TAPS)]
                dve.wait_ge(s_freed, 4 * (G_CONV + g) + j + 1)
                link(nc.vector.tensor_scalar(tile4[:, j, :], vpad[:, j, 0:SEQ], tap[0], None, ALU.mult))
                link(nc.vector.scalar_tensor_tensor(tile4[:, j, :], vpad[:, j, 1:1 + SEQ], tap[1], tile4[:, j, :], ALU.mult, ALU.add))
                link(nc.vector.scalar_tensor_tensor(tile4[:, j, :], vpad[:, j, 2:2 + SEQ], tap[2], tile4[:, j, :], ALU.mult, ALU.add))
                link(nc.vector.tensor_tensor(tile4[:, j, :], tile4[:, j, :], rbc[:, :], ALU.mult))

            def y_out_(g, j):
                done(G_CONV + g, j)
                nc.vector.tensor_tensor(tile4[:, j, :], B[j][:, :], tile4[:, j, :], ALU.mult).then_inc(s_freed, 1)

            def y_more(g, j):
                ct = 4 * (g // 3) + j
                dve.wait_ge(s_chi, ct + 1)
                nc.vector.tensor_tensor(conv_t[:, ct, 1, :], tile4[:, j, :], conv_t[:, ct, 0, :], ALU.subtract).then_inc(s_clo, 1)

            outs, more = (c_out, v_out, y_out_), (c_more, v_more, y_more)

            def conv_out(g):
                for j in range(4):
                    outs[g % 3](g, j)

            for g in range(6):
                for k in range(KT):
                    lo(B_CONV + KT * g, 0, None, k, gmix)
                    if g == 0 and 3 <= k < 7:
                        qkv_out(2, k - 3)
                    if g == 0 and k == 8:
                        link(nc.vector.memset(vpad[:, :, 0:2], 0.0))
                    if g and (g - 1) % 3 != 2 and k in (4, 6, 8, 10):
                        more[(g - 1) % 3](g - 1, k // 2 - 2)
                    if g == 3 and 11 <= k < 15:
                        y_more(2, k - 11)
                    if k % 2:
                        slot = KT // 2 * g + k // 2
                        if 0 <= slot - 9 < UNITS:
                            normalised(slot - 9)
                        if 0 <= slot - 12 < UNITS:
                            heads_lo(slot - 12)
                        if g and k == 1:
                            conv_out(g - 1)
                        if 0 <= slot - 8 < UNITS:
                            masked(slot - 8)

            def gate_out(g, per=0, i=None):
                def f(j):
                    done(g, j, per, i)
                    nc.vector.tensor_tensor(tile4[:, j, :], banks(g)[j][:, :], rbc[:, :], ALU.mult).then_inc(s_freed, 1)
                return f

            def branch_out(g, first, gates, t, per=0, gper=0, i=None):
                def f(j):
                    done(g, j, per, i)
                    dve.wait_ge(s_gate, gates + j + 1 + (i * gper if i is not None else 0))
                    dst = acc[:, t + j, :] if i is None else acc[:, bass.ds(i * 4 + t + j, 1), :].rearrange("p a n -> p (a n)")
                    nc.vector.tensor_tensor(dst if first else tile4[:, j, :], banks(g)[j][:, :], tile4[:, j, :],
                                            ALU.mult).then_inc(s_freed, 1)
                    if not first:
                        out_of(g, j, per, i)
                        nc.vector.tensor_tensor(dst, dst, tile4[:, j, :], ALU.add).then_inc(s_mg, 1)
                return f

            M, G = B_MERGE, G_MERGE
            for k in range(KT):
                lo(M, 0, None, k, gmix)
                if k == 3:
                    conv_out(5)
                if 8 <= k < 12:
                    y_more(5, k - 8)
            with dve.Fori(0, 3) as i:
                b, per = M + KT, MERGE_BLOCKS
                group(b, CT, None, per, i, gate_out(G, 16, i))
                group(b + CT, KT, gmix, per, i, branch_out(G + 1, True, 0, 0, 16, 8, i))
                group(b + CT + KT, CT, None, per, i, gate_out(G + 2, 16, i))
                group(b + 2 * CT + KT, KT, gmix, per, i, branch_out(G + 3, False, 4, 0, 16, 8, i))
            M += 3 * MERGE_BLOCKS
            G += 12

            def merged_lo(k):
                dve.wait_ge(s_mhi, k + 1)
                nc.vector.tensor_tensor(mrg_t[:, k, 1, :], acc[:, k, :], mrg_t[:, k, 0, :], ALU.subtract).then_inc(s_mlo, 1)

            group(M + KT, CT, None, after=gate_out(G))
            for k in range(KT):
                lo(M + KT + CT, 0, None, k, gmix)
                if 3 <= k < 7:
                    branch_out(G + 1, True, 24, 12)(k - 3)
                if k >= 10:
                    merged_lo(k - 10)
            for k in range(6, 8):
                merged_lo(k)
            group(M + 2 * KT + CT, CT, None, after=gate_out(G + 2))

            def h_sum(g, t, j, dst):
                done(g, j)
                nc.vector.tensor_tensor(dst, banks(g)[j][:, :], h_hi[:, t % KT, :], ALU.add).then_inc(s_freed, 1)
                dve.wait_ge(s_freed, 4 * g + j + 1)
                nc.vector.tensor_tensor(dst, dst, h_lo[:, t % KT, :], ALU.add).then_inc(s_hs, 1)

            def h_split(t, src, sq):
                dve.wait_ge(s_hhi, t + 1)
                nc.vector.tensor_tensor(h_lo[:, t % KT, :], src, h_hi[:, t % KT, :], ALU.subtract).then_inc(s_hlo, 1)
                if t % KT == 0:
                    nc.vector.tensor_copy(ssq[:, :], sq).then_inc(s_hs, 1)
                else:
                    dve.wait_ge(s_hs, 2 * t)
                    nc.vector.tensor_tensor(ssq[:, :], ssq[:, :], sq, ALU.add).then_inc(s_hs, 1)

            def residual(g, c, t0, dst, sq):
                def f(j):
                    t = t0 + 4 * c + j
                    h_sum(g, t, j, dst(4 * c + j, j))
                    h_split(t, dst(4 * c + j, j), sq(j))
                return f

            for k in range(KT):
                lo(B_WOUT, 0, None, k)
                if 3 <= k < 7:
                    branch_out(G + 3, False, 28, 12)(k - 3)
                if k >= 8:
                    merged_lo(k)
            w_dst, w_sq = (lambda t, j: tile4[:, j, :]), (lambda j: acc[:, 12 + j, :])
            for c in range(1, 4):
                group(B_WOUT + KT * c, KT, after=residual(G_WOUT + c - 1, c - 1, 0, w_dst, w_sq))
                if c == 3:
                    dve.wait_ge(s_ssm, MT)
                    link(rsqrt(2, rmem[:, :], rtm2[:, :], rtp[:, 0:MT], ssm[:, :]))
                    for t in range(MT):
                        nc.vector.tensor_scalar(mem_n[:, t, :], mem_n[:, t, :], rmem[:, t:t + 1], None, ALU.mult).then_inc(s_mn, 1)

            def rstd_rows(n, bk, var, tmp):
                dve.wait_ge(s_rT, n)
                rsqrt(n + 1, rbc[:, :], var, tmp, bk[:, :]).then_inc(s_rbc, 1)
                dve.wait_ge(s_rbc, n)

            def mem_lo(m):
                t, kg = divmod(m, 4)
                dve.wait_ge(s_mthi, m + 1)
                ks, ts = slice(4 * kg, 4 * kg + 4), slice(t * P, (t + 1) * P)
                nc.vector.tensor_tensor(mem_t[:, ks, 1, ts], B[m % 4][:, :].rearrange("p (k q) -> p k q", k=4),
                                        mem_t[:, ks, 0, ts], ALU.subtract).then_inc(s_mtlo, 1)
            for k in range(KT):
                lo(B_XQ, 0, None, k, gx)
                if 3 <= k < 7:
                    residual(G_WOUT + 3, 3, 0, w_dst, w_sq)(k - 3)
                if k == 12:
                    rstd_rows(2, B[0], acc[:, 8, :], acc[:, 9, :])
                if k >= 12:
                    for m in range(2 * (k - 12), 2 * (k - 12) + 2):
                        mem_lo(m)


            def xq_out(j):
                done(G_XQ, j)
                nc.vector.tensor_tensor(xq_t[:, j, :], banks(G_XQ)[j][:, :], rbc[:, :], ALU.mult).then_inc(s_freed, 1)

            def kx_out(j):
                done(G_XK, j)
                nc.vector.tensor_copy(kx[:, j, :], banks(G_XK)[j][:, 0:NMEM]).then_inc(s_freed, 1)

            def x_max(u):
                dve.wait_ge(s_xs, u + 1)
                link(nc.vector.tensor_reduce(st_x[:, 0, u:u + 1], B[u % 2][:, 0:NMEM], mybir.AxisListType.X, ALU.max))
                nc.vector.tensor_scalar(st_x[:, 1, u:u + 1], st_x[:, 0, u:u + 1], -(XHD ** -0.5), None, ALU.mult).then_inc(s_xm, 1)

            def x_norm(u):
                dve.wait_ge(s_xe, u + 1)
                link(nc.vector.reciprocal(st_x[:, 3, u:u + 1], st_x[:, 2, u:u + 1]))
                nc.vector.tensor_scalar(px[:, u, :], px[:, u, :], st_x[:, 3, u:u + 1], None, ALU.mult).then_inc(s_xp, 1)

            group(B_XK, KT, gm, after=xq_out)
            for k in range(KT):
                lo(B_XV, 0, None, k, gm)
                if k == 3:
                    for j in range(4):
                        kx_out(j)
                if k >= 4:
                    x_max(k - 4)
                if k >= 5:
                    x_norm(k - 5)
            for u in range(12, 16):
                x_max(u)
                x_norm(u - 1)
            x_norm(15)
            for k in range(XH):
                lo(B_XO, 0, None, k)
            for j in range(MT):
                done(G_XV, 2 * j + 1)
                nc.vector.tensor_copy(vx[:, j, :], banks(G_XV)[j][:, :]).then_inc(s_freed, 2)
            for h in range(XH):
                dve.wait_ge(s_xohi, h + 1)
                nc.vector.tensor_tensor(xo_t[:, h, 1, :], A[2 + h % 2][:, :], xo_t[:, h, 0, :], ALU.subtract).then_inc(s_xolo, 1)
            x_dst, x_sq_ = (lambda t, j: acc[:, t, :]), (lambda j: tile4[:, j, :])
            for c in range(1, 4):
                group(B_XO + XH * c, XH, after=residual(G_XO + c - 1, c - 1, KT, x_dst, x_sq_))

            def first_gate(j):
                residual(G_XO + 3, 3, KT, x_dst, x_sq_)(j)

            for k in range(KT):
                lo(B_G0, 0, None, k, gf)
                if 3 <= k < 7:
                    first_gate(k - 3)
                if k == 12:
                    rstd_rows(3, A[0], up[:, 0, :], up[:, 1, :])

            def hidden_out(g, gates, n0, per=0, i=None):
                def f(j):
                    done(g, j, per, i)
                    dve.wait_ge(s_gate, gates + j + 1 + (i * 4 if i is not None else 0))
                    nc.vector.tensor_tensor(up[:, j, :], banks(g)[j][:, :], rbc[:, :], ALU.mult).then_inc(s_freed, 1)
                    out_of(g, j, per, i)
                    nc.vector.tensor_tensor(tile4[:, j, :], up[:, j, :], tile4[:, j, :], ALU.mult).then_inc(s_upp, 1)
                    dve.wait_ge(s_ahi, n0 + j + 1 + (i * 4 if i is not None else 0))
                    nc.vector.tensor_tensor(act_t[:, j, 1, :], tile4[:, j, :], act_t[:, j, 0, :], ALU.subtract).then_inc(s_alo, 1)
                return f

            def down_out(g, c, per=0, i=None):
                def f(j):
                    done(g, j, per, i)
                    t = 4 * c + j
                    nc.vector.tensor_tensor(acc[:, t, :], acc[:, t, :], banks(g)[j][:, :], ALU.add).then_inc(s_freed, 1)
                return f

            group(B_U0, KT, gf, after=gate_out(G_G0))
            with dve.Fori(0, FG - 1) as i:
                b, per = B_FFN, FFN_BLOCKS
                group(b, KT, gf, per, i, hidden_out(G_FFN - 1, 32, 0, 24, i))
                group(b + KT, 4, None, per, i, gate_out(G_FFN, 24, i))
                for c in range(1, 4):
                    group(b + KT + 4 * c, 4, None, per, i, down_out(G_FFN + c, c - 1, 24, i))
                group(b + 2 * KT, KT, gf, per, i, down_out(G_FFN + 4, 3, 24, i))
            group(B_LAST, 4, after=hidden_out(G_LAST - 1, 32 + 4 * (FG - 1), 4 * (FG - 1)))

            def last_out(g, c):
                def f(j):
                    t = 4 * c + j
                    done(g, j)
                    nc.vector.tensor_tensor(acc[:, t, :], acc[:, t, :], banks(g)[j][:, :], ALU.add).then_inc(s_freed, 1)
                    dve.wait_ge(s_hhi, 2 * KT + t + 1)
                    if t == 0:
                        nc.vector.tensor_copy(ssq[:, :], tile4[:, j, :]).then_inc(s_fsq, 1)
                    else:
                        dve.wait_ge(s_fsq, t)
                        nc.vector.tensor_tensor(ssq[:, :], ssq[:, :], tile4[:, j, :], ALU.add).then_inc(s_fsq, 1)
                return f

            for c in range(1, 4):
                group(B_LAST + 4 * c, 4, after=last_out(G_LAST + c - 1, c - 1))
            for j in range(4):
                last_out(G_LAST + 3, 3)(j)
            FB = banks(G_LAST)
            dve.wait_ge(s_fs, 1)
            rsqrt(5, rcol[:, :], rtm[:, :], rtp[:, :], FB[0][:, 0:TT]).then_inc(s_fr, 1)
            dve.wait_ge(s_fr, 1)
            dve.wait_ge(s_gfin, 16)
            for m in range(TT * 4):
                t, kg = divmod(m, 4)
                bk = bank[(m + 1) % 8] if FB is A else bank[(m + 5) % 8]
                dve.wait_ge(s_fT, m + 1)
                f = slice(512 * kg, 512 * kg + 512)
                nc.vector.scalar_tensor_tensor(y_out[:, t, f], bk[:, :], rcol[:, t:t + 1], gfin[:, f],
                                               ALU.mult, ALU.mult).then_inc(s_y, 1)


_INS = ["x", "mem", "g_mix", "w_in", "conv_w", "sinks", "w_attn_o", "w_conv_o", "w_out", "g_xattn", "g_mem",
        "w_xq", "w_xkv", "w_xo", "g_ffn", "w_gate_up", "w_down", "g_final"]


def kernel(**inputs):
    import concourse.bacc as bacc
    from concourse.bass_utils import run_bass_kernel_spmd

    nc = bacc.Bacc("TRN2", target_bir_lowering=False, num_devices=1)
    arrays, args = {}, []
    for name in _INS:
        a = np.ascontiguousarray(inputs[name])
        arrays[f"in_{name}_dram"] = a
        args.append(nc.dram_tensor(f"in_{name}_dram", a.shape, mybir.dt.from_np(a.dtype), kind="ExternalInput").ap())
    arrays["rope_dram"] = rope_table()
    args.append(nc.dram_tensor("rope_dram", (SEQ, 2 * HALF), F32, kind="ExternalInput").ap())
    args.append(nc.dram_tensor("out_0_dram", (1, SEQ, D), F32, kind="ExternalOutput").ap())
    build(nc, *args)
    r = run_bass_kernel_spmd(nc, [arrays], core_ids=[0])
    return r.results[0]["out_0_dram"]
```

```python
from contextlib import ExitStack

import numpy as np

import concourse.bass as bass
from concourse import mybir

F32 = mybir.dt.float32
F32R = mybir.dt.float32r
ACT = mybir.ActivationFunctionType
ALU = mybir.AluOpType

P = 128
D = 2048
SEQ = 512
NMEM = 256
KT = D // P
TT = SEQ // P
MT = NMEM // P
HD = 64
NQ = 16
NKV = 4
PAIRS = NQ // 2
ROT = HD // 4
HALF = ROT // 2
THETA = 500000.0
CONV = D // 2
CT = CONV // P
TAPS = 3
XH = 4
XHD = 128
FF = -(-8 * D // (3 * 256)) * 256
FG = FF // 512
EPS = 1e-6
NEG = -3.0e38

Q0 = 0
K0 = NQ * HD
CB0 = K0 + 2 * NKV * HD
CC0 = CB0 + CONV
CH0 = CC0 + CONV
GA0 = CH0 + CONV
GC0 = GA0 + D

B_QKV = 0
B_CONV = B_QKV + 3 * KT
B_MERGE = B_CONV + 6 * KT
MERGE_BLOCKS = 2 * KT + 2 * CT
B_WOUT = B_MERGE + 4 * MERGE_BLOCKS
B_XQ = B_WOUT + 4 * KT
B_XK = B_XQ + KT
B_XV = B_XK + KT
B_XO = B_XV + KT
B_G0 = B_XO + 4 * XH
B_U0 = B_G0 + KT
B_FFN = B_U0 + KT
FFN_BLOCKS = 3 * KT
B_LAST = B_FFN + (FG - 1) * FFN_BLOCKS

G_QKV = 0
G_CONV = 3
G_MERGE = 9
G_WOUT = G_MERGE + 16
G_XQ = G_WOUT + 4
G_XK = G_XQ + 1
G_XV = G_XK + 1
G_XO = G_XV + 1
G_G0 = G_XO + 4
G_U0 = G_G0 + 1
G_FFN = G_U0 + 1
G_LAST = G_FFN + 6 * (FG - 1)

RAW = 4
SPL = 4
XUNITS = XH * TT
UNITS = PAIRS * TT


def x_units(k):
    first = [(3 * max(b - 1, 0) + 1) // 2 for b in (k, k + 1)]
    return range(min(first[0], XUNITS), min(first[1], XUNITS)) if k >= 1 else range(0)


def rope_table():
    inv = (THETA ** (-np.arange(0, ROT, 2, dtype=np.float32) / np.float32(ROT))).astype(np.float32)
    ang = np.arange(SEQ, dtype=np.float32)[:, None] * inv[None, :]
    return np.concatenate([np.cos(ang), np.sin(ang)], axis=1).astype(np.float32)


def build(nc, x, mem, g_mix, w_in, conv_w, sinks, w_attn_o, w_conv_o, w_out, g_xattn, g_mem,
          w_xq, w_xkv, w_xo, g_ffn, w_gate_up, w_down, g_final, rope, out):
    with ExitStack() as ctx:
        def sem(name):
            return ctx.enter_context(nc.semaphore(name))

        KB = 1024
        base = -(-nc.sbuf_base // 32) * 32
        size = 200 * KB + 7552
        ctx.enter_context(nc.sbuf_tensor("arena", [P, size + base - nc.sbuf_base], mybir.dt.uint8))

        def at(name, off, shape, dt=F32):
            return nc.alloc_sbuf_tensor_at(name, shape, dt, offset=base + off)

        h_hi = at("h_hi", 0, [P, KT, SEQ], F32R)
        h_lo = at("h_lo", 32 * KB, [P, KT, SEQ], F32R)
        raw = at("raw", 64 * KB, [P, RAW, 2, 512])
        w_hi = at("w_hi", 80 * KB, [P, SPL, 512], F32R)
        w_lo = at("w_lo", 88 * KB, [P, SPL, 512], F32R)
        x_sq = at("x_sq", 96 * KB, [P, D])
        k_hi = at("k_hi", 96 * KB, [P, NKV, SEQ], F32R)
        k_lo = at("k_lo", 104 * KB, [P, NKV, SEQ], F32R)
        v_hi = at("v_hi", 112 * KB, [P, TT, NKV, 2, HD], F32R)
        v_lo = at("v_lo", 120 * KB, [P, TT, NKV, 2, HD], F32R)
        acc = at("acc", 96 * KB, [P, KT, SEQ])
        mem_n = at("mem_n", 96 * KB, [P, MT, D])
        mem_sq = at("mem_sq", 112 * KB, [P, D])
        x_nat = at("x_nat", 128 * KB, [P, TT, D])
        conv_t = at("conv_t", 128 * KB, [P, CT, 2, SEQ], F32R)
        stage = at("stage", 128 * KB, [P, TT, 8, HD])
        kdup = at("kdup", 136 * KB, [P, TT, NKV, 2, HD])
        rtmp = at("rtmp", 152 * KB, [P, 4, 8, HALF])
        probs = at("probs", 144 * KB, [P, 3, 2, 256])
        v_c = at("v_c", 150 * KB, [P, 4, SEQ])
        pt_lo = at("pt_lo", 158 * KB, [P, 2, 2, P], F32R)
        q_s = at("q_s", 160 * KB, [P, PAIRS, 2, SEQ], F32R)
        attn_t = at("attn_t", 160 * KB, [P, PAIRS, 2, SEQ], F32R)
        mrg_t = at("mrg_t", 128 * KB, [P, KT, 2, SEQ], F32R)
        mem_t = at("mem_t", 128 * KB, [P, KT, 2, NMEM], F32R)
        xo_t = at("xo_t", 128 * KB, [P, XH, 2, SEQ], F32R)
        xq_t = at("xq_t", 160 * KB, [P, XH, SEQ])
        kx = at("kx", 168 * KB, [P, XH, NMEM])
        vx = at("vx", 172 * KB, [P, MT, XH * XHD])
        px = at("px", 176 * KB, [P, XUNITS, NMEM])
        act_t = at("act_t", 144 * KB, [P, 4, 2, SEQ], F32R)
        up = at("up", 160 * KB, [P, 4, SEQ])
        gfin = at("gfin", 176 * KB, [P, D])
        y_out = at("y_out", 0, [P, TT, D])
        tile4 = at("tile4", 192 * KB, [P, 4, SEQ])
        pt_x = at("pt_x", 96 * KB, [P, XH, MT, SEQ])
        o = 200 * KB
        rbc = at("rbc", o, [P, SEQ]); o += 2 * KB
        pt_hi = at("pt_hi", o, [P, 2, 2, P], F32R); ssq = at("ssq", o, [P, SEQ]); o += 2 * KB
        mask = at("mask", o, [P, 256]); o += KB
        ident = at("ident", o, [P, P]); o += 512
        ones = at("ones", o, [P, P]); o += 512
        prow = at("prow", 192 * KB, [88, P])
        par = at("par", o, [P, 88]); o += 352
        cs = at("cs", o, [P, TT, 2, HALF]); o += 256
        snk = at("snk", o, [P, NQ]); nsnk = at("nsnk", o + 64, [P, NQ]); o += 128
        ssx = at("ssx", o, [P, TT])
        rcol = at("rcol", o + 32, [P, TT])
        rtm = at("rtm", o + 64, [P, TT])
        ssm = at("ssm", o + 96, [P, MT])
        rmem = at("rmem", o + 128, [P, MT])
        rtm2 = at("rtm2", o + 160, [P, MT])
        rtp = at("rtp", o + 192, [P, TT])
        o += 224
        st_a = at("st_a", o, [P, 4, 6, 2])
        o += 192
        st_x = at("st_x", o, [P, 4, XUNITS])
        o += 256
        gmix, gx, gm, gf = (par[:, KT * i:KT * i + KT] for i in range(4))
        assert o <= size, o

        bank = [ctx.enter_context(nc.psum_tensor(f"bank{i}", [P, 512], F32)) for i in range(8)]
        A, B = bank[0:4], bank[4:8]

        def banks(g):
            if g < G_MERGE:
                return B if g >= G_CONV or g == 1 else A
            return A if g % 2 else B

        s_x = [sem(f"x_loaded{t}") for t in range(TT)]
        s_prow = sem("gains_loaded")
        s_small = sem("rope_sinks_loaded")
        s_mem = sem("mem_loaded")
        s_gfin = sem("gfinal_loaded")
        s_const0 = sem("constants_cleared")
        s_const = sem("constants_ready")
        s_raw = [sem(f"raw_loaded{i}") for i in range(RAW)]
        s_hi = sem("weights_hi_ready")
        s_lo = sem("weights_lo_ready")
        s_used = sem("weights_used")
        s_done = sem("bank_done")
        s_freed = sem("bank_freed")
        s_parT = sem("gains_transposed")
        s_par = sem("gains_ready")
        s_xT = sem("x_transposed")
        s_xhi = sem("x_hi_ready")
        s_xlo = sem("x_lo_ready")
        s_ssx = sem("x_squares_ready")
        s_rcol = sem("x_rstd_ready")
        s_rT = sem("rstd_broadcast")
        s_rbc = sem("rbc_ready")
        s_stage = sem("qkv_stage_ready")
        s_tr = sem("qkv_transposed")
        s_qhi = sem("qk_hi_ready")
        s_qkv = sem("qkv_ready")
        s_s = sem("scores_done")
        s_sm = sem("masked_scores_ready")
        s_e = sem("exp_done")
        s_p = sem("probs_ready")
        s_pT = sem("probs_transposed")
        s_pthi = sem("probs_t_hi_ready")
        s_pts = sem("probs_t_ready")
        s_o = sem("heads_done")
        s_ohi = sem("heads_hi_ready")
        s_olo = sem("heads_lo_ready")
        s_chi = sem("conv_hi_ready")
        s_clo = sem("conv_lo_ready")
        s_gate = sem("gate_ready")
        s_mg = sem("merged_tiles")
        s_mhi = sem("merged_hi_ready")
        s_mlo = sem("merged_lo_ready")
        s_hs = sem("h_sum_ready")
        s_hhi = sem("h_hi_ready")
        s_hlo = sem("h_lo_ready")
        s_sqr = sem("squares_ready")
        s_sqa = sem("squares_added")
        s_sum = sem("squares_summed")
        s_ssm = sem("mem_squares_ready")
        s_mn = sem("mem_normalised")
        s_mT = sem("mem_transposed")
        s_mthi = sem("mem_hi_ready")
        s_mtlo = sem("mem_lo_ready")
        s_xs = sem("xscores_done")
        s_xm = sem("xmax_ready")
        s_xe = sem("xexp_done")
        s_xp = sem("xprobs_ready")
        s_xpT = sem("xprobs_transposed")
        s_xpt = sem("xprobs_t_ready")
        s_xoo = sem("xheads_done")
        s_xohi = sem("xheads_hi_ready")
        s_xolo = sem("xheads_lo_ready")
        s_upp = sem("hidden_ready")
        s_ahi = sem("hidden_hi_ready")
        s_alo = sem("hidden_lo_ready")
        s_fT = sem("final_transposed")
        s_y = sem("y_ready")
        s_out = sem("out_stored")
        s_var = sem("variance_ready")
        s_root = sem("root_ready")
        s_v = sem("vector_step")

        block = ctx.enter_context(nc.Block())

        @block.sync
        def _(sp):
            sp.dma_start(x_nat[:, 0, :], x[0, 0:P, :]).then_inc(s_x[0], 16)
            for i, g in enumerate((g_mix, g_xattn, g_mem, g_ffn)):
                sp.dma_start(prow[KT * i:KT * i + KT, :], g.rearrange("l (k p) -> (l k) p", p=P)).then_inc(s_prow, 16)
            sp.dma_start(prow[4 * KT:4 * KT + TAPS * CT, :],
                         conv_w.rearrange("l t (k p) -> (l t k) p", p=P)).then_inc(s_prow, 16)
            for t in range(1, TT):
                sp.dma_start(x_nat[:, t, :], x[0, t * P:(t + 1) * P, :]).then_inc(s_x[t], 16)

            def load(n0, per, i, c, w, row, col):
                n = n0 + c
                free = 2 * (n - RAW) + 2
                if i is None:
                    if n >= RAW:
                        sp.wait_ge(s_lo, free)
                    src = w[row:row + 256, col:col + 512].rearrange("(b p) n -> p b n", p=P)
                    sp.dma_start(raw[:, n % RAW, :, :], src).then_inc(s_raw[n % RAW], 16)
                else:
                    need = sp.to_reg(i * (2 * per) + free)
                    src = w[bass.ds(row, 256), bass.ds(col, 512)].rearrange("(b p) n -> p b n", p=P)
                    sp.dma_start(raw[:, n % RAW, :, :], src).wait_op(s_lo, need, "sem-ge").then_inc(s_raw[n % RAW], 16)

            wi, wc, wa, wo = w_in[0], w_conv_o[0], w_attn_o[0], w_out[0]
            for g, col in enumerate((Q0, Q0 + 512, K0)):
                for c in range(KT // 2):
                    load(B_QKV // 2 + 8 * g, 0, None, c, wi, 256 * c, col)
                    if g == 0 and c == RAW - 1:
                        sp.dma_start(cs[:, :, :, :].rearrange("p t a e -> p t (a e)"),
                                     rope.rearrange("(t p) e -> p t e", p=P)).then_inc(s_small, 16)
                        sp.dma_start(snk[:, :], sinks.partition_broadcast(P)[:, 0, :]).then_inc(s_small, 16)
            with sp.Fori(0, 2) as i:
                for g, col in enumerate((CC0, CH0, CB0)):
                    for c in range(KT // 2):
                        load(B_CONV // 2 + 8 * g, 24, i, c, wi, 256 * c, i * 512 + col)
            with sp.Fori(0, 4) as i:
                n = B_MERGE // 2
                for w, col, chunks in ((wi, GC0, 8), (wc, 0, 4), (wi, GA0, 8), (wa, 0, 4)):
                    for c in range(chunks):
                        load(n, MERGE_BLOCKS // 2, i, c, w, 256 * c, i * 512 + col)
                    n += chunks
            with sp.Fori(0, 4) as i:
                for c in range(8):
                    load(B_WOUT // 2, 8, i, c, wo, 256 * c, i * 512)
            for n, w, col in ((B_XQ, w_xq[0], 0), (B_XK, w_xkv[0], 0), (B_XV, w_xkv[0], 512)):
                for c in range(8):
                    load(n // 2, 0, None, c, w, 256 * c, col)
            for g in range(4):
                for c in range(2):
                    load(B_XO // 2 + 2 * g, 0, None, c, w_xo[0], 256 * c, 512 * g)
            wgu, wd = w_gate_up[0], w_down[0]
            for c in range(8):
                load(B_G0 // 2, 0, None, c, wgu, 256 * c, 0)
            for c in range(8):
                load(B_U0 // 2, 0, None, c, wgu, 256 * c, FF)
            with sp.Fori(0, FG - 1) as i:
                for c in range(8):
                    load(B_FFN // 2, 24, i, c, wgu, 256 * c, i * 512 + 512)
                for g in range(4):
                    for c in range(2):
                        load(B_FFN // 2 + 8 + 2 * g, 24, i, c, wd, i * 512 + 256 * c, 512 * g)
                for c in range(8):
                    load(B_FFN // 2 + 16, 24, i, c, wgu, 256 * c, i * 512 + FF + 512)
            for g in range(4):
                for c in range(2):
                    load(B_LAST // 2 + 2 * g, 0, None, c, wd, (FG - 1) * 512 + 256 * c, 512 * g)
            for m in range(2 * TT):
                t, f = m // 2, slice((m % 2) * (D // 2), (m % 2 + 1) * (D // 2))
                sp.wait_ge(s_y, 2 * (m + 1))
                sp.dma_start(out[0, t * P:(t + 1) * P, f], y_out[:, t, f]).then_inc(s_out, 16)
            sp.wait_ge(s_out, 16 * 2 * TT)

        @block.gpsimd
        def _(pool):
            pool.memset(ident[:, :], 0.0).then_inc(s_const0, 1)
            pool.memset(mask[:, :], 0.0).then_inc(s_const0, 1)
            pool.memset(ones[:, :], 1.0).then_inc(s_const, 1)
            pool.wait_ge(s_const0, 2)
            pool.affine_select(out=ident[:, :], in_=ident[:, :], compare_op=ALU.not_equal, fill=1.0,
                               base=0, pattern=[[-1, P]], channel_multiplier=1).then_inc(s_const, 1)
            pool.affine_select(out=mask[:, :], in_=mask[:, :], compare_op=ALU.is_gt, fill=NEG,
                               base=0, pattern=[[1, 256]], channel_multiplier=-1).then_inc(s_const0, 1)
            pool.wait_ge(s_const0, 3)
            pool.affine_select(out=mask[:, :], in_=mask[:, :], compare_op=ALU.is_ge, fill=NEG,
                               base=P, pattern=[[-1, 256]], channel_multiplier=1).then_inc(s_const, 1)
            pool.wait_ge(s_mlo, KT)
            pool.dma_start(mem_n[:, :, :], mem[0].rearrange("(t p) n -> p t n", p=P)).then_inc(s_mem, 16)
            pool.wait_ge(s_done, 4 * G_G0 + 1)
            pool.dma_start(gfin[:, :], g_final.partition_broadcast(P)).then_inc(s_gfin, 16)

        @block.tensor
        def _(pe):
            def wait_block(b0, per, i, k):
                pe.wait_ge(s_lo, b0 + k + 1 + (i * per if i is not None else 0))

            def columns(bk, k, n, hi, lo, width=SEQ, wait_bank=None):
                s = k % SPL
                for j in range(4):
                    if k == 0 and wait_bank:
                        wait_bank(j)
                    c = slice(j * P, (j + 1) * P)
                    o_ = bk[j][:, 0:width]
                    pe.matmul(o_, w_hi[:, s, c], hi, start=(k == 0), stop=False)
                    pe.matmul(o_, w_hi[:, s, c], lo, start=False, stop=False)
                    mm = pe.matmul(o_, w_lo[:, s, c], hi, start=False, stop=(k == n - 1))
                    if k == n - 1:
                        mm.then_inc(s_done, 1)
                if k < n - 1:
                    mm.then_inc(s_used, 1)

            def rows(bk, k, n, hi, lo, tiles, inc, wait_bank=None):
                s = k % SPL
                for j in range(tiles):
                    if k == 0 and wait_bank:
                        wait_bank(j)
                    c = slice(j * P, (j + 1) * P)
                    pe.matmul(bk[j][:, :], hi[:, c], w_hi[:, s, :], start=(k == 0), stop=False)
                    pe.matmul(bk[j][:, :], hi[:, c], w_lo[:, s, :], start=False, stop=False)
                    mm = pe.matmul(bk[j][:, :], lo[:, c], w_hi[:, s, :], start=False, stop=(k == n - 1))
                    if k == n - 1:
                        mm.then_inc(s_done, inc)
                if k < n - 1:
                    mm.then_inc(s_used, 1)

            def freed(g, per=0, i=None):
                return lambda j: pe.wait_ge(s_freed, 4 * (g - 2) + j + 1 + (i * per if i is not None else 0))

            def square_sums(bk, n):
                pe.wait_ge(s_sqa, n)
                for t in range(TT):
                    mm = pe.matmul(bk[:, t:t + 1], ssq[:, t * P:(t + 1) * P], ones[:, 0:1], start=True, stop=True)
                mm.then_inc(s_sum, 1)

            def broadcast_rstd(bk, n):
                pe.wait_ge(s_rcol, n)
                for t in range(TT):
                    mm = pe.matmul(bk[:, t * P:(t + 1) * P], rcol[:, t:t + 1].to_broadcast([P, P]), ident[:, :],
                                   start=True, stop=True)
                mm.then_inc(s_rT, 1)

            pe.wait_ge(s_const, 3)
            for m in range(TT * 4):
                t, kg = divmod(m, 4)
                if kg == 0:
                    pe.wait_ge(s_x[t], 16)
                if m >= 8:
                    pe.wait_ge(s_xlo, m - 7)
                for q in range(4):
                    k = 4 * kg + q
                    mm = pe.transpose(bank[m % 8][:, q * P:(q + 1) * P], x_nat[:, t, k * P:(k + 1) * P], ident[:, :])
                mm.then_inc(s_xT, 1)
                if m == 3:
                    pe.wait_ge(s_prow, 80)
                    pe.transpose(bank[7][:, 0:88], prow[:, :], ident[0:88, 0:88]).then_inc(s_parT, 1)
                if m == 6:
                    pe.wait_ge(s_par, 1)

            def qkv_transposes(g, t):
                pe.wait_ge(s_stage, 4 * g + t + 1)
                src = stage[:, t, :, :].rearrange("p h d -> p (h d)") if g < 2 else kdup[:, t, :, :, :].rearrange("p h a d -> p (h a d)")
                for q in range(4):
                    mm = pe.transpose(banks(g)[t][:, q * P:(q + 1) * P], src[:, q * P:(q + 1) * P], ident[:, :])
                mm.then_inc(s_tr, 1)

            for g in range(3):
                for k in range(KT):
                    wait_block(B_QKV + KT * g, 0, None, k)
                    if g == 0 and k == 0:
                        pe.wait_ge(s_xlo, 16)
                    if g == 1 and k == 0:
                        pe.wait_ge(s_rbc, 1)
                    if g == 2 and k == 0:
                        pe.wait_ge(s_qkv, 4)
                    rows(banks(g), k, KT, h_hi[:, k, :], h_lo[:, k, :], TT, 1)
                    if g == 0 and k == 13:
                        broadcast_rstd(B[0], 1)
                    if g and 6 <= k < 10:
                        qkv_transposes(g - 1, k - 6)

            S0, S1, PT, O = A

            def scores(u):
                p, n = divmod(u, TT)
                c0 = 0 if n else P
                pe.wait_ge(s_qkv, 12)
                if u:
                    pe.wait_ge(s_sm, u)
                for e in range(2):
                    r = slice(HD * e, HD * e + HD)
                    q, ks = slice(n * P, (n + 1) * P), slice((n - 1) * P + c0, (n + 1) * P)
                    pe.matmul((S0, S1)[e][:, c0:256], q_s[:, p, e, q], k_hi[:, p // 2, ks], start=True, stop=False)
                    mm = pe.matmul((S0, S1)[e][:, c0:256], q_s[r, p, e, q], k_lo[r, p // 2, ks], start=False, stop=True)
                mm.then_inc(s_s, 1)

            def probs_transposes(u):
                n = u % TT
                pe.wait_ge(s_p, u + 1)
                if u:
                    pe.wait_ge(s_pts, u)
                else:
                    pe.wait_ge(s_qkv, 12)
                for c in range(0 if n else 1, 2):
                    for e in range(2):
                        mm = pe.transpose(PT[:, (2 * c + e) * P:(2 * c + e + 1) * P],
                                          probs[:, u % 3, e, c * P:(c + 1) * P], ident[:, :])
                mm.then_inc(s_pT, 1)

            def heads(u):
                p, n = divmod(u, TT)
                pe.wait_ge(s_pts, u + 1)
                if u:
                    pe.wait_ge(s_olo, u)
                first, c0 = True, 0 if n else 1
                for c in range(c0, 2):
                    v_h, v_l = (v[:, n - 1 + c, p // 2, :, :].rearrange("p a d -> p (a d)") for v in (v_hi, v_lo))
                    for v, pt in ((v_h, pt_hi), (v_h, pt_lo), (v_l, pt_hi)):
                        mm = pe.matmul(O[:, 0:256], v, pt[:, c, :, :].rearrange("p e q -> p (e q)"), start=first,
                                       stop=(c == 1 and v is v_l))
                        first = False
                mm.then_inc(s_o, 1)

            for g in range(6):
                for k in range(KT):
                    wait_block(B_CONV + KT * g, 0, None, k)
                    if g == 0 and k == 0:
                        pe.wait_ge(s_qkv, 8)

                    def wb(j):
                        if g:
                            pe.wait_ge(s_freed, 4 * (G_CONV + g - 1) + j + 1)
                    columns(B, k, KT, h_hi[:, k, :], h_lo[:, k, :], wait_bank=wb)
                    if g == 0 and 6 <= k < 10:
                        qkv_transposes(2, k - 6)
                    slot = KT // 2 * g + k // 2
                    if k % 2 == 0:
                        if 0 <= slot - 11 < UNITS:
                            heads(slot - 11)
                    else:
                        if 0 <= slot - 7 < UNITS:
                            scores(slot - 7)
                        if 0 <= slot - 9 < UNITS:
                            probs_transposes(slot - 9)

            pe.wait_ge(s_olo, UNITS)
            with pe.Fori(0, 4) as i:
                b, g = B_MERGE, G_MERGE
                for kind in range(4):
                    n = KT if kind % 2 == 0 else CT
                    for k in range(n):
                        wait_block(b, MERGE_BLOCKS, i, k)
                        if kind % 2 == 0:
                            hi, lo = h_hi[:, k, :], h_lo[:, k, :]
                        else:
                            if kind == 1:
                                pe.wait_ge(s_clo, k + 1)
                            src = conv_t if kind == 1 else attn_t
                            hi, lo = src[:, k, 0, :], src[:, k, 1, :]
                        columns(banks(g), k, n, hi, lo, wait_bank=freed(g, 16, i))
                    b += n
                    g += 1
            with pe.Fori(0, 2) as i:
                for c in range(2):
                    for k in range(KT):
                        wait_block(B_WOUT + KT * c, 2 * KT, i, k)
                        pe.wait_ge(s_mlo, k + 1)
                        columns(banks(G_WOUT + c), k, KT, mrg_t[:, k, 0, :], mrg_t[:, k, 1, :],
                                wait_bank=freed(G_WOUT + c, 8, i))
            for k in range(KT):
                wait_block(B_XQ, 0, None, k)
                pe.wait_ge(s_hlo, k + 1)
                columns(banks(G_XQ), k, KT, h_hi[:, k, :], h_lo[:, k, :], wait_bank=freed(G_XQ))
                if k == 9:
                    square_sums(B[0], KT)
                if k == 12:
                    broadcast_rstd(B[0], 2)
                if 10 <= k < 14:
                    for m in range(2 * (k - 10), 2 * (k - 10) + 2):
                        kg, t = divmod(m, MT)
                        if m == 0:
                            pe.wait_ge(s_mn, MT)
                        if m >= 3:
                            pe.wait_ge(s_mtlo, m - 2)
                        for q in range(4):
                            mm = pe.transpose(B[1 + m % 3][:, q * P:(q + 1) * P],
                                              mem_n[:, t, (4 * kg + q) * P:(4 * kg + q + 1) * P], ident[:, :])
                        mm.then_inc(s_mT, 1)
            for k in range(KT):
                wait_block(B_XK, 0, None, k)
                if k == 0:
                    pe.wait_ge(s_mtlo, 8)
                    pe.wait_ge(s_rbc, 2)
                columns(banks(G_XK), k, KT, mem_t[:, k, 0, :], mem_t[:, k, 1, :], width=NMEM)

            def x_scores(u):
                h, t = divmod(u, TT)
                if u == 0:
                    pe.wait_ge(s_freed, 4 * G_XK + 4)
                if u >= 4:
                    pe.wait_ge(s_xe, u - 3)
                pe.matmul(B[u % 4][:, 0:NMEM], xq_t[:, h, t * P:(t + 1) * P], kx[:, h, :],
                          start=True, stop=True).then_inc(s_xs, 1)

            def x_transposes(h):
                for c in range(MT):
                    if h:
                        pe.wait_ge(s_xpt, 2 * (h - 1) + c + 1)
                    else:
                        pe.wait_ge(s_freed, 4 * G_XQ + 3 + c)
                    for t in range(TT):
                        pe.wait_ge(s_xp, TT * h + t + 1)
                        mm = pe.transpose(A[2 + c][:, t * P:(t + 1) * P], px[:, TT * h + t, c * P:(c + 1) * P], ident[:, :])
                    mm.then_inc(s_xpT, 1)

            for k in range(KT):
                wait_block(B_XV, 0, None, k)
                rows(banks(G_XV), k, KT, mem_t[:, k, 0, :], mem_t[:, k, 1, :], MT, 2, wait_bank=freed(G_XV))
                for u in x_units(k):
                    x_scores(u)
                for u in x_units(k - 4):
                    if u % TT == TT - 1:
                        x_transposes(u // TT)
            for h in range(XH):
                if h == 0:
                    pe.wait_ge(s_freed, 4 * G_XV + 4)
                pe.wait_ge(s_xpt, 2 * h + 2)
                for c in range(MT):
                    mm = pe.matmul(B[h][:, :], vx[:, c, h * XHD:(h + 1) * XHD], pt_x[:, h, c, :],
                                   start=(c == 0), stop=(c == MT - 1))
                mm.then_inc(s_xoo, 1)
            for c in range(4):
                for k in range(XH):
                    wait_block(B_XO + XH * c, 0, None, k)
                    pe.wait_ge(s_xolo, k + 1)

                    def wb(j):
                        if c == 0:
                            pe.wait_ge(s_xolo, j + 1)
                        if c >= 2:
                            pe.wait_ge(s_freed, 4 * (G_XO + c - 2) + j + 1)
                    columns(banks(G_XO + c), k, XH, xo_t[:, k, 0, :], xo_t[:, k, 1, :], wait_bank=wb)

            def hidden(g, b, per_g, per_b, i, norm=False):
                for k in range(KT):
                    wait_block(b, per_b, i, k)
                    if norm:
                        pe.wait_ge(s_hlo, KT + k + 1)
                    columns(banks(g), k, KT, h_hi[:, k, :], h_lo[:, k, :], wait_bank=freed(g, per_g, i))
                    if norm and k == 12:
                        square_sums(A[0], 2 * KT)
                    if norm and k == 14:
                        broadcast_rstd(A[0], 3)

            def down(g, b, alo, per_g, per_b, i):
                for c in range(4):
                    for k in range(4):
                        wait_block(b + 4 * c, per_b, i, k)
                        if c == 0:
                            pe.wait_ge(s_alo, alo + k + 1 + (i * 4 if i is not None else 0))
                        columns(banks(g + c), k, 4, act_t[:, k, 0, :], act_t[:, k, 1, :], wait_bank=freed(g + c, per_g, i))

            hidden(G_G0, B_G0, 0, 0, None, norm=True)
            pe.wait_ge(s_rbc, 3)
            hidden(G_U0, B_U0, 0, 0, None)
            with pe.Fori(0, FG - 1) as i:
                hidden(G_FFN, B_FFN, 24, FFN_BLOCKS, i)
                down(G_FFN + 1, B_FFN + KT, 0, 24, FFN_BLOCKS, i)
                hidden(G_FFN + 5, B_FFN + 2 * KT, 24, FFN_BLOCKS, i)
            down(G_LAST, B_LAST, 4 * (FG - 1), 0, 0, None)

            FB = banks(G_LAST)
            square_sums(FB[0], 3 * KT)
            for m in range(TT * 4):
                t, kg = divmod(m, 4)
                bk = bank[(m + 1) % 8] if FB is A else bank[(m + 5) % 8]
                if m >= 7:
                    pe.wait_ge(s_y, m - 7 if m > 7 else 1)
                if m == 7:
                    pe.wait_ge(s_rcol, 4)
                if m >= 8:
                    pe.wait_ge(s_y, m - 7)
                for q in range(4):
                    mm = pe.transpose(bk[:, q * P:(q + 1) * P], acc[:, 4 * kg + q, t * P:(t + 1) * P], ident[:, :])
                mm.then_inc(s_fT, 1)

        @block.scalar
        def _(act):
            def hi(b0, g, k, gain=None, per=0, gper=0, i=None):
                n = (b0 + k) // 2
                s = (b0 + k) % SPL
                if k % 2 == 0:
                    act.wait_ge(s_raw[n % RAW], 16 * (n // RAW + 1) + (i * (2 * per) if i is not None else 0))
                if k == SPL - 1 and g:
                    act.wait_ge(s_done, 4 * g + (i * (4 * gper) if i is not None else 0))
                elif b0 + k >= SPL:
                    before = g if k >= SPL else g - 1
                    act.wait_ge(s_used, b0 + k - SPL + 1 - before + (i * (per - gper) if i is not None else 0))
                sc = 1.0 if gain is None else gain[:, k:k + 1]
                nc.scalar.activation(w_hi[:, s, :], raw[:, n % RAW, (b0 + k) % 2, :], ACT.Copy, scale=sc).then_inc(s_hi, 1)

            def group(b0, g, n, gain=None, per=0, gper=0, i=None, after=None):
                for k in range(n):
                    hi(b0, g, k, gain, per, gper, i)
                    if after and n > 4 and 4 <= k < 8:
                        after(k - 4)
                if after and n <= 4:
                    for j in range(4):
                        after(j)

            for m in range(TT * 4):
                t, kg = divmod(m, 4)
                act.wait_ge(s_xT, m + 1)
                nc.scalar.activation(h_hi[:, 4 * kg:4 * kg + 4, t * P:(t + 1) * P],
                                     bank[m % 8][:, :].rearrange("p (k q) -> p k q", k=4), ACT.Copy).then_inc(s_xhi, 1)
                if m == 4:
                    act.wait_ge(s_parT, 1)
                    nc.scalar.activation(par[:, :], bank[7][:, 0:88], ACT.Copy).then_inc(s_par, 1)
                    act.wait_ge(s_par, 1)

            def root(n, dst, var):
                act.wait_ge(s_var, n)
                nc.scalar.activation(dst, var, ACT.Sqrt).then_inc(s_root, 1)

            def qk_hi(g, t):
                act.wait_ge(s_tr, 4 * g + t + 1)
                src, ts = banks(g)[t][:, :].rearrange("p (k q) -> p k q", k=4), slice(t * P, (t + 1) * P)
                if g < 2:
                    for e in range(2):
                        r = slice(HD * e, HD * e + HD)
                        last = nc.scalar.activation(q_s[r, 4 * g:4 * g + 4, e, ts], src[r], ACT.Copy)
                else:
                    nc.scalar.activation(k_hi[:, :, ts], src, ACT.Copy)
                    for a in range(2):
                        last = nc.scalar.activation(v_hi[:, t, :, a, :], stage[:, t, NKV:2 * NKV, :], ACT.Copy)
                last.then_inc(s_qhi, 1)

            for g in range(3):
                for k in range(KT):
                    hi(B_QKV + KT * g, G_QKV + g, k, gmix)
                    if g == 0 and 4 <= k < 8:
                        if k > 4:
                            act.wait_ge(s_ssx, k - 4)
                        nc.scalar.activation(x_sq[:, :], x_nat[:, k - 4, :], ACT.Square,
                                             accum_out=ssx[:, k - 4:k - 3]).then_inc(s_ssx, 1)
                    if g == 0 and k == 10:
                        root(1, rcol[:, :], rtm[:, :])
                    if g and 10 <= k < 14:
                        qk_hi(g - 1, k - 10)

            def exps(u):
                r, n = u % 3, u % TT
                s, c0 = st_a[:, u % 4], 0 if n else P
                act.wait_ge(s_sm, u + 1)
                for e in range(2):
                    nc.scalar.activation(probs[:, r, e, c0:256], probs[:, r, e, c0:256], ACT.Exp, bias=s[:, 1, e:e + 1],
                                         accum_out=s[:, 2, e:e + 1])
                nc.scalar.activation(s[:, 3, :], s[:, 4, :], ACT.Exp).then_inc(s_e, 1)

            def probs_out(u):
                act.wait_ge(s_pT, u + 1)
                if u:
                    act.wait_ge(s_o, u)
                c0 = 0 if u % TT else 1
                nc.scalar.activation(pt_hi[:, c0:2, :, :].rearrange("p c e q -> p (c e q)"),
                                     PT_[:, 256 * c0:512], ACT.Copy).then_inc(s_pthi, 1)

            def heads_hi(u):
                p, n = divmod(u, TT)
                act.wait_ge(s_o, u + 1)
                for e in range(2):
                    r = slice(HD * e, HD * e + HD)
                    last = nc.scalar.activation(attn_t[r, p, 0, n * P:(n + 1) * P], O_[r, e * P:(e + 1) * P], ACT.Copy)
                last.then_inc(s_ohi, 1)

            PT_, O_ = A[2], A[3]
            for g in range(6):
                for k in range(KT):
                    hi(B_CONV + KT * g, G_CONV + g, k, gmix)
                    if g == 0 and 10 <= k < 14:
                        qk_hi(2, k - 10)
                    if g == 3 and 8 <= k < 12:
                        act.wait_ge(s_freed, 4 * (G_CONV + 2) + k - 7)
                        nc.scalar.activation(conv_t[:, k - 8, 0, :], tile4[:, k - 8, :], ACT.Copy).then_inc(s_chi, 1)
                    slot = KT // 2 * g + k // 2
                    if k % 2 == 0:
                        if 0 <= slot - 13 < UNITS:
                            heads_hi(slot - 13)
                        if 0 <= slot - 12 < UNITS:
                            probs_out(slot - 12)
                    elif 0 <= slot - 9 < UNITS:
                        exps(slot - 9)

            def conv_hi(j):
                act.wait_ge(s_freed, 4 * (G_CONV + 5) + j + 1)
                nc.scalar.activation(conv_t[:, 4 + j, 0, :], tile4[:, j, :], ACT.Copy).then_inc(s_chi, 1)

            def gate(g, func, gper=0, i=None):
                def f(j):
                    act.wait_ge(s_freed, 4 * g + j + 1 + (i * (4 * gper) if i is not None else 0))
                    nc.scalar.activation(tile4[:, j, :], tile4[:, j, :], func).then_inc(s_gate, 1)
                return f

            def merged_hi(k):
                if k == 0:
                    act.wait_ge(s_done, 4 * (G_MERGE + 13) + 4)
                if k == 8:
                    act.wait_ge(s_done, 4 * (G_MERGE + 15) + 4)
                if k >= 8:
                    act.wait_ge(s_mg, k + 1)
                nc.scalar.activation(mrg_t[:, k, 0, :], acc[:, k, :], ACT.Copy).then_inc(s_mhi, 1)

            M, G, MB = B_MERGE, G_MERGE, MERGE_BLOCKS
            group(M, G, KT, gmix, after=conv_hi)
            with act.Fori(0, 3) as i:
                group(M + KT, G + 1, CT, None, MB, 4, i, gate(G, ACT.Sigmoid, 4, i))
                group(M + KT + CT, G + 2, KT, gmix, MB, 4, i)
                group(M + 2 * KT + CT, G + 3, CT, None, MB, 4, i, gate(G + 2, ACT.Sigmoid, 4, i))
                group(M + MB, G + 4, KT, gmix, MB, 4, i)
            M += 3 * MB
            G += 12
            group(M + KT, G + 1, CT, after=gate(G, ACT.Sigmoid))
            act.wait_ge(s_mg, 8)
            for k in range(KT):
                hi(M + KT + CT, G + 2, k, gmix)
                if k >= 8:
                    merged_hi(k - 8)
            group(M + 2 * KT + CT, G + 3, CT, after=gate(G + 2, ACT.Sigmoid))

            def h_part(t, src):
                act.wait_ge(s_hs, t + 1)
                nc.scalar.activation(h_hi[:, t % KT, :], src, ACT.Copy).then_inc(s_hhi, 1)

            def square(t, src, dst):
                if t % KT >= 4:
                    act.wait_ge(s_sqa, t - 3)
                nc.scalar.activation(dst, src, ACT.Square).then_inc(s_sqr, 1)

            def wout_after(t):
                j = t % 4
                h_part(t, tile4[:, j, :])
                square(t, tile4[:, j, :], acc[:, 12 + j, :])

            for k in range(KT):
                hi(B_WOUT, G_WOUT, k)
                if k >= 6 and k < 14:
                    merged_hi(k + 2)
            for c in range(1, 4):
                for k in range(KT):
                    hi(B_WOUT + KT * c, G_WOUT + c, k)
                    if k in (4, 6, 8, 10):
                        wout_after(4 * (c - 1) + k // 2 - 2)
                    if c == 3 and k in (5, 11):
                        t = k // 11
                        if t:
                            act.wait_ge(s_ssm, t)
                        else:
                            act.wait_ge(s_mem, 16)
                        nc.scalar.activation(mem_sq[:, :], mem_n[:, t, :], ACT.Square, accum_out=ssm[:, t:t + 1]).then_inc(s_ssm, 1)
                    if c == 3 and k == 13:
                        root(2, rmem[:, :], rtm2[:, :])

            def mem_hi(m):
                kg, t = divmod(m, MT)
                act.wait_ge(s_mT, m + 1)
                nc.scalar.activation(mem_t[:, 4 * kg:4 * kg + 4, 0, t * P:(t + 1) * P],
                                     B[1 + m % 3][:, :].rearrange("p (k q) -> p k q", k=4), ACT.Copy).then_inc(s_mthi, 1)

            def rbc_out(bk, n):
                act.wait_ge(s_rT, n)
                nc.scalar.activation(rbc[:, :], bk[:, :], ACT.Copy).then_inc(s_rbc, 1)

            for k in range(KT):
                hi(B_XQ, G_XQ, k, gx)
                if k in (4, 6, 8, 10):
                    wout_after(12 + k // 2 - 2)
                if k == 13:
                    root(3, rcol[:, :], rtm[:, :])
                if k >= 13:
                    mem_hi(2 * (k - 13))
                    mem_hi(2 * (k - 13) + 1)
                if k == 15:
                    rbc_out(B[0], 2)
            for k in range(KT):
                hi(B_XK, G_XK, k, gm)
                if k == 0:
                    mem_hi(6)
                    mem_hi(7)

            def x_exp(u):
                act.wait_ge(s_xm, u + 1)
                nc.scalar.activation(px[:, u, :], B[u % 4][:, 0:NMEM], ACT.Exp, bias=st_x[:, 1, u:u + 1],
                                     scale=XHD ** -0.5, accum_out=st_x[:, 2, u:u + 1]).then_inc(s_xe, 1)

            def probs_after(k):
                for u in x_units(k - 8):
                    if u % TT == TT - 1:
                        h = u // TT
                        for c in range(MT):
                            act.wait_ge(s_xpT, 2 * h + c + 1)
                            nc.scalar.activation(pt_x[:, h, c, :], A[2 + c][:, :], ACT.Copy).then_inc(s_xpt, 1)

            for k in range(KT):
                hi(B_XV, G_XV, k, gm)
                for u in x_units(k - 4):
                    x_exp(u)
                probs_after(k)
            for k in range(XH - 1):
                hi(B_XO, G_XO, k)
                probs_after(KT + k)
            act.wait_ge(s_done, 4 * G_XV + 4)
            nc.scalar.activation(vx[:, 1, :], banks(G_XV)[1][:, :], ACT.Copy).then_inc(s_freed, 2)
            hi(B_XO, G_XO, XH - 1)
            probs_after(KT + XH - 1)
            for h in range(XH):
                act.wait_ge(s_xoo, h + 1)
                nc.scalar.activation(xo_t[:, h, 0, :], B[h][:, :], ACT.Copy).then_inc(s_xohi, 1)
            for n in range(4, 16):
                hi(B_XO + n // 4 * 4, G_XO + n // 4, n % 4)
                if n >= 7:
                    h_part(KT + n - 7, acc[:, n - 7, :])
            for k in range(KT):
                hi(B_G0, G_G0, k, gf)
                if k < 7:
                    h_part(KT + 9 + k, acc[:, 9 + k, :])
                if 6 <= k < 14:
                    for t in (2 * (k - 6), 2 * (k - 6) + 1):
                        square(KT + t, acc[:, t, :], tile4[:, t % 4, :])

            def hidden_hi(n0, i=None):
                def f(j):
                    act.wait_ge(s_upp, n0 + j + 1 + (i * 4 if i is not None else 0))
                    nc.scalar.activation(act_t[:, j, 0, :], tile4[:, j, :], ACT.Copy).then_inc(s_ahi, 1)
                return f

            for k in range(KT):
                hi(B_U0, G_U0, k, gf)
                if k == 0:
                    root(4, rcol[:, :], rtm[:, :])
                if k == 2:
                    rbc_out(A[0], 3)
                if 4 <= k < 8:
                    gate(G_G0, ACT.Silu)(k - 4)
            with act.Fori(0, FG - 1) as i:
                b, g, per = B_FFN, G_FFN, FFN_BLOCKS
                group(b, g, KT, gf, per, 6, i, hidden_hi(0, i))
                group(b + KT, g + 1, 4, None, per, 6, i, gate(g, ACT.Silu, 6, i))
                for c in range(1, 4):
                    group(b + KT + 4 * c, g + 1 + c, 4, None, per, 6, i)
                group(b + 2 * KT, g + 5, KT, gf, per, 6, i)
            for k in range(4):
                if k == 3:
                    hidden_hi(4 * (FG - 1))(0)
                hi(B_LAST, G_LAST, k)
            for j in range(1, 4):
                hidden_hi(4 * (FG - 1))(j)

            def f_sq(c):
                def f(j):
                    act.wait_ge(s_freed, 4 * (G_LAST + c) + j + 1)
                    square(2 * KT + 4 * c + j, acc[:, 4 * c + j, :], tile4[:, j, :])
                return f

            for c in range(1, 4):
                group(B_LAST + 4 * c, G_LAST + c, 4, after=f_sq(c - 1))
            nc.scalar.activation(rtm2[:, :], rmem[:, :], ACT.Sqrt)
            for j in range(4):
                f_sq(3)(j)
            root(5, rcol[:, :], rtm[:, :])

        @block.vector
        def _(dve):
            step = [0]

            def link(ins):
                ins.then_inc(s_v, 1)
                step[0] += 1
                dve.wait_ge(s_v, step[0])

            def rsqrt(n, dst, var, tmp, total):
                nc.vector.tensor_scalar(var, total, 1.0 / D, EPS, ALU.mult, ALU.add).then_inc(s_var, 1)
                dve.wait_ge(s_root, n)
                link(nc.vector.reciprocal(dst, dst))
                link(nc.vector.tensor_tensor(tmp, dst, dst, ALU.mult))
                link(nc.vector.tensor_tensor(tmp, tmp, var, ALU.mult))
                link(nc.vector.tensor_scalar(tmp, tmp, -0.5, 1.5, ALU.mult, ALU.add))
                return nc.vector.tensor_tensor(dst, dst, tmp, ALU.mult)

            def lo(b0, per, i, k, g=None):
                n = (b0 + k) // 2
                s = (b0 + k) % SPL
                dve.wait_ge(s_hi, b0 + k + 1 + (i * per if i is not None else 0))
                src = raw[:, n % RAW, (b0 + k) % 2, :]
                if g is None:
                    nc.vector.tensor_tensor(w_lo[:, s, :], src, w_hi[:, s, :], ALU.subtract).then_inc(s_lo, 1)
                else:
                    nc.vector.scalar_tensor_tensor(w_lo[:, s, :], src, g[:, k:k + 1], w_hi[:, s, :],
                                                   ALU.mult, ALU.subtract).then_inc(s_lo, 1)

            def group(b0, n, g=None, per=0, i=None, after=None):
                for k in range(n):
                    lo(b0, per, i, k, g)
                    if after and n > 4 and 3 <= k < 7:
                        after(k - 3)
                if after and n <= 4:
                    for j in range(4):
                        after(j)

            def out_of(g, j, per=0, i=None):
                dve.wait_ge(s_freed, 4 * g + j + 1 + (i * per if i is not None else 0))

            def done(g, j, per=0, i=None):
                dve.wait_ge(s_done, 4 * g + j + 1 + (i * per if i is not None else 0))

            for m in range(TT * 4):
                t, kg = divmod(m, 4)
                dve.wait_ge(s_xhi, m + 1)
                sl = (slice(None), slice(4 * kg, 4 * kg + 4), slice(t * P, (t + 1) * P))
                nc.vector.tensor_tensor(h_lo[sl], bank[m % 8][:, :].rearrange("p (k q) -> p k q", k=4), h_hi[sl],
                                        ALU.subtract).then_inc(s_xlo, 1)

            def rotate(v, nh, t):
                t1, t2 = v[:, :, 0:HALF], v[:, :, HALF:ROT]
                cos = cs[:, t, 0, :].unsqueeze(1).to_broadcast([P, nh, HALF])
                sin = cs[:, t, 1, :].unsqueeze(1).to_broadcast([P, nh, HALF])
                r = rtmp
                nc.vector.tensor_tensor(r[:, 0, 0:nh, :], t1, cos, ALU.mult)
                nc.vector.tensor_tensor(r[:, 1, 0:nh, :], t2, sin, ALU.mult)
                nc.vector.tensor_tensor(r[:, 2, 0:nh, :], t2, cos, ALU.mult)
                link(nc.vector.tensor_tensor(r[:, 3, 0:nh, :], t1, sin, ALU.mult))
                nc.vector.tensor_tensor(t1, r[:, 0, 0:nh, :], r[:, 1, 0:nh, :], ALU.subtract)
                return nc.vector.tensor_tensor(t2, r[:, 2, 0:nh, :], r[:, 3, 0:nh, :], ALU.add)

            def qkv_out(g, t):
                done(g, t)
                if g:
                    dve.wait_ge(s_tr, 4 * (g - 1) + t + 1)
                ps = banks(g)[t]
                nc.vector.tensor_scalar(stage[:, t, :, :].rearrange("p h d -> p (h d)"), ps[:, :], rcol[:, t:t + 1],
                                        None, ALU.mult).then_inc(s_freed, 1)
                out_of(g, t)
                if g < 2:
                    rotate(stage[:, t, :, :], 8, t).then_inc(s_stage, 1)
                else:
                    link(rotate(stage[:, t, 0:NKV, :], NKV, t))
                    for a in range(2):
                        last = nc.vector.tensor_copy(kdup[:, t, :, a, :], stage[:, t, 0:NKV, :])
                    last.then_inc(s_stage, 1)

            for k in range(KT):
                lo(B_QKV, 0, None, k, gmix)
                if k == 9:
                    dve.wait_ge(s_ssx, TT)
                    rsqrt(1, rcol[:, :], rtm[:, :], rtp[:, :], ssx[:, :]).then_inc(s_rcol, 1)
                    dve.wait_ge(s_rcol, 1)
                    dve.wait_ge(s_small, 32)
                    link(nc.vector.tensor_scalar(nsnk[:, :], snk[:, :], -1.0, None, ALU.mult))
            dve.wait_ge(s_rT, 1)
            nc.vector.tensor_copy(rbc[:, :], B[0][:, :]).then_inc(s_rbc, 1)
            def qk_lo(g, t):
                dve.wait_ge(s_qhi, 4 * g + t + 1)
                src, ts = banks(g)[t][:, :].rearrange("p (k q) -> p k q", k=4), slice(t * P, (t + 1) * P)
                if g < 2:
                    for e in range(2):
                        r, other = slice(HD * e, HD * e + HD), slice(HD * (1 - e), HD * (1 - e) + HD)
                        last = nc.vector.tensor_tensor(q_s[other, 4 * g:4 * g + 4, e, ts], src[r],
                                                       q_s[r, 4 * g:4 * g + 4, e, ts], ALU.subtract)
                else:
                    nc.vector.tensor_tensor(k_lo[:, :, ts], src, k_hi[:, :, ts], ALU.subtract)
                    for a in range(2):
                        last = nc.vector.tensor_tensor(v_lo[:, t, :, a, :], stage[:, t, NKV:2 * NKV, :], v_hi[:, t, :, a, :],
                                                       ALU.subtract)
                last.then_inc(s_qkv, 1)

            for g in (1, 2):
                for k in range(KT):
                    lo(B_QKV + KT * g, 0, None, k, gmix)
                    if 3 <= k < 7:
                        qkv_out(g - 1, k - 3)
                    if 11 <= k < 15:
                        qk_lo(g - 1, k - 11)

            def masked(u):
                p, n = divmod(u, TT)
                s, c0 = st_a[:, u % 4], 0 if n else P
                dve.wait_ge(s_s, u + 1)
                if u >= 3:
                    dve.wait_ge(s_pT, u - 2)
                for e in range(2):
                    ins = nc.vector.tensor_tensor_reduce(out=probs[:, u % 3, e, c0:256], in0=A[e][:, c0:256], in1=mask[:, c0:256],
                                                         scale=HD ** -0.5, scalar=NEG, op0=ALU.add, op1=ALU.max,
                                                         accum_out=s[:, 0, e:e + 1])
                link(ins)
                link(nc.vector.scalar_tensor_tensor(s[:, 1, :], s[:, 0, :], -1.0, nsnk[:, 2 * p:2 * p + 2], ALU.mult, ALU.min))
                nc.vector.tensor_tensor(s[:, 4, :], s[:, 1, :], snk[:, 2 * p:2 * p + 2], ALU.add).then_inc(s_sm, 1)

            def normalised(u):
                s, c0 = st_a[:, u % 4], 0 if u % TT else P
                dve.wait_ge(s_e, u + 1)
                link(nc.vector.tensor_tensor(s[:, 5, :], s[:, 2, :], s[:, 3, :], ALU.add))
                link(nc.vector.reciprocal(s[:, 5, :], s[:, 5, :]))
                for e in range(2):
                    ins = nc.vector.tensor_scalar(probs[:, u % 3, e, c0:256], probs[:, u % 3, e, c0:256], s[:, 5, e:e + 1], None, ALU.mult)
                ins.then_inc(s_p, 1)

            def probs_lo(u):
                dve.wait_ge(s_pthi, u + 1)
                c0 = 0 if u % TT else 1
                nc.vector.tensor_tensor(pt_lo[:, c0:2, :, :].rearrange("p c e q -> p (c e q)"), A[2][:, 256 * c0:512],
                                        pt_hi[:, c0:2, :, :].rearrange("p c e q -> p (c e q)"), ALU.subtract).then_inc(s_pts, 1)

            def heads_lo(u):
                p, n = divmod(u, TT)
                dve.wait_ge(s_ohi, u + 1)
                for e in range(2):
                    r = slice(HD * e, HD * e + HD)
                    q = slice(n * P, (n + 1) * P)
                    ins = nc.vector.tensor_tensor(attn_t[r, p, 1, q], A[3][r, e * P:(e + 1) * P], attn_t[r, p, 0, q], ALU.subtract)
                ins.then_inc(s_olo, 1)

            def c_out(g, j):
                done(G_CONV + g, j)
                nc.vector.tensor_tensor(tile4[:, j, :], B[j][:, :], rbc[:, :], ALU.mult).then_inc(s_freed, 1)

            def c_more(g, j):
                dve.wait_ge(s_freed, 4 * (G_CONV + g) + j + 1)
                link(nc.vector.tensor_tensor(tile4[:, j, :], tile4[:, j, :], rbc[:, :], ALU.mult))

            def v_out(g, j):
                done(G_CONV + g, j)
                nc.vector.tensor_tensor(v_c[:, j, :], B[j][:, :], tile4[:, j, :], ALU.mult).then_inc(s_freed, 1)

            def taps(g, j, first):
                ct = 4 * (g // 3) + j
                tap = [par[:, 4 * KT + CT * a + ct:4 * KT + CT * a + ct + 1] for a in range(TAPS)]

                def back_by(b):
                    now = tile4[:, j, b:SEQ]
                    link(nc.vector.scalar_tensor_tensor(now, v_c[:, j, 0:SEQ - b], tap[2 - b], now, ALU.mult, ALU.add))

                if first:
                    dve.wait_ge(s_freed, 4 * (G_CONV + g) + j + 1)
                    link(nc.vector.tensor_scalar(tile4[:, j, :], v_c[:, j, :], tap[2], None, ALU.mult))
                    back_by(1)
                else:
                    back_by(2)
                    link(nc.vector.tensor_tensor(tile4[:, j, :], tile4[:, j, :], rbc[:, :], ALU.mult))

            def y_out_(g, j):
                done(G_CONV + g, j)
                nc.vector.tensor_tensor(tile4[:, j, :], B[j][:, :], tile4[:, j, :], ALU.mult).then_inc(s_freed, 1)

            def y_more(g, j):
                ct = 4 * (g // 3) + j
                dve.wait_ge(s_chi, ct + 1)
                nc.vector.tensor_tensor(conv_t[:, ct, 1, :], tile4[:, j, :], conv_t[:, ct, 0, :], ALU.subtract).then_inc(s_clo, 1)

            outs = (c_out, v_out, y_out_)

            def conv_out(g):
                for j in range(4):
                    outs[g % 3](g, j)

            for g in range(6):
                for k in range(KT):
                    lo(B_CONV + KT * g, 0, None, k, gmix)
                    if g == 0 and 3 <= k < 7:
                        qkv_out(2, k - 3)
                    if g == 0 and 11 <= k < 15:
                        qk_lo(2, k - 11)
                    slot = KT // 2 * g + k // 2
                    if k % 2 == 0:
                        if 0 <= slot - 13 < UNITS:
                            heads_lo(slot - 13)
                        if 0 <= slot - 12 < UNITS:
                            probs_lo(slot - 12)
                    else:
                        if 0 <= slot - 9 < UNITS:
                            masked(slot - 9)
                        if 0 <= slot - 10 < UNITS:
                            normalised(slot - 10)
                    if g and k == 2:
                        conv_out(g - 1)
                    if g % 3 == 1 and k in (4, 6, 8, 10):
                        c_more(g - 1, k // 2 - 2)
                    if g % 3 == 2 and 4 <= k < 12:
                        taps(g - 1, k // 2 - 2, k % 2 == 0)
                    if g == 3 and 11 <= k < 15:
                        y_more(2, k - 11)

            def gate_out(g, per=0, i=None):
                def f(j):
                    done(g, j, per, i)
                    if g == G_G0:
                        dve.wait_ge(s_rbc, 3)
                    nc.vector.tensor_tensor(tile4[:, j, :], banks(g)[j][:, :], rbc[:, :], ALU.mult).then_inc(s_freed, 1)
                return f

            def branch_out(g, first, gates, t, per=0, gper=0, i=None):
                def f(j):
                    done(g, j, per, i)
                    dve.wait_ge(s_gate, gates + j + 1 + (i * gper if i is not None else 0))
                    dst = acc[:, t + j, :] if i is None else acc[:, bass.ds(i * 4 + t + j, 1), :].rearrange("p a n -> p (a n)")
                    nc.vector.tensor_tensor(dst if first else tile4[:, j, :], banks(g)[j][:, :], tile4[:, j, :],
                                            ALU.mult).then_inc(s_freed, 1)
                    if not first:
                        out_of(g, j, per, i)
                        nc.vector.tensor_tensor(dst, dst, tile4[:, j, :], ALU.add).then_inc(s_mg, 1)
                return f

            M, G = B_MERGE, G_MERGE
            for k in range(KT):
                lo(M, 0, None, k, gmix)
                if k == 3:
                    conv_out(5)
                if 8 <= k < 12:
                    y_more(5, k - 8)
            with dve.Fori(0, 3) as i:
                b, per = M + KT, MERGE_BLOCKS
                group(b, CT, None, per, i, gate_out(G, 16, i))
                group(b + CT, KT, gmix, per, i, branch_out(G + 1, True, 0, 0, 16, 8, i))
                group(b + CT + KT, CT, None, per, i, gate_out(G + 2, 16, i))
                group(b + 2 * CT + KT, KT, gmix, per, i, branch_out(G + 3, False, 4, 0, 16, 8, i))
            M += 3 * MERGE_BLOCKS
            G += 12

            def merged_lo(k):
                dve.wait_ge(s_mhi, k + 1)
                nc.vector.tensor_tensor(mrg_t[:, k, 1, :], acc[:, k, :], mrg_t[:, k, 0, :], ALU.subtract).then_inc(s_mlo, 1)

            group(M + KT, CT, None, after=gate_out(G))
            for k in range(KT):
                lo(M + KT + CT, 0, None, k, gmix)
                if 3 <= k < 7:
                    branch_out(G + 1, True, 24, 12)(k - 3)
                if k >= 10:
                    merged_lo(k - 10)
            for k in range(6, 8):
                merged_lo(k)
            group(M + 2 * KT + CT, CT, None, after=gate_out(G + 2))

            def h_sum(g, t, dst):
                j = t % 4
                done(g, j)
                nc.vector.tensor_tensor(dst, banks(g)[j][:, :], h_hi[:, t % KT, :], ALU.add).then_inc(s_freed, 1)
                dve.wait_ge(s_freed, 4 * g + j + 1)
                nc.vector.tensor_tensor(dst, dst, h_lo[:, t % KT, :], ALU.add).then_inc(s_hs, 1)

            def h_part(t, src):
                dve.wait_ge(s_hhi, t + 1)
                nc.vector.tensor_tensor(h_lo[:, t % KT, :], src, h_hi[:, t % KT, :], ALU.subtract).then_inc(s_hlo, 1)

            def add_square(t, sq):
                dve.wait_ge(s_sqr, t + 1)
                if t % KT == 0:
                    nc.vector.tensor_copy(ssq[:, :], sq).then_inc(s_sqa, 1)
                else:
                    dve.wait_ge(s_sqa, t)
                    nc.vector.tensor_tensor(ssq[:, :], ssq[:, :], sq, ALU.add).then_inc(s_sqa, 1)

            def wout_after(c, k):
                if k in (5, 7, 9, 11):
                    t = 4 * c + (k - 5) // 2
                    h_part(t, tile4[:, t % 4, :])
                    add_square(t, acc[:, 12 + t % 4, :])
                if k in (3, 5, 7, 9):
                    t = 4 * c + (k - 3) // 2
                    h_sum(G_WOUT + c, t, tile4[:, t % 4, :])

            for k in range(KT):
                lo(B_WOUT, 0, None, k)
                if 3 <= k < 7:
                    branch_out(G + 3, False, 28, 12)(k - 3)
                if k >= 8:
                    merged_lo(k)
            for c in range(1, 4):
                for k in range(KT):
                    lo(B_WOUT + KT * c, 0, None, k)
                    wout_after(c - 1, k)
                    if c == 3 and k == 12:
                        dve.wait_ge(s_ssm, MT)
                        link(rsqrt(2, rmem[:, :], rtm2[:, :], rtp[:, 0:MT], ssm[:, :]))
                    if c == 3 and k >= 14:
                        t = k - 14
                        nc.vector.tensor_scalar(mem_n[:, t, :], mem_n[:, t, :], rmem[:, t:t + 1], None, ALU.mult).then_inc(s_mn, 1)

            def rstd(n, bk):
                dve.wait_ge(s_sum, n)
                rsqrt(n + 2, rcol[:, :], rtm[:, :], rtp[:, :], bk[:, 0:TT]).then_inc(s_rcol, 1)
                dve.wait_ge(s_rcol, n + 1)

            def mem_lo(m):
                kg, t = divmod(m, MT)
                dve.wait_ge(s_mthi, m + 1)
                ks, ts = slice(4 * kg, 4 * kg + 4), slice(t * P, (t + 1) * P)
                nc.vector.tensor_tensor(mem_t[:, ks, 1, ts], B[1 + m % 3][:, :].rearrange("p (k q) -> p k q", k=4),
                                        mem_t[:, ks, 0, ts], ALU.subtract).then_inc(s_mtlo, 1)

            for k in range(KT):
                lo(B_XQ, 0, None, k, gx)
                wout_after(3, k)
                if k == 12:
                    rstd(1, B[0])
                if k >= 13:
                    mem_lo(2 * (k - 13))
                    mem_lo(2 * (k - 13) + 1)

            def xq_out(j):
                done(G_XQ, j)
                if j == 0:
                    dve.wait_ge(s_rbc, 2)
                nc.vector.tensor_tensor(xq_t[:, j, :], banks(G_XQ)[j][:, :], rbc[:, :], ALU.mult).then_inc(s_freed, 1)

            def kx_out(j):
                done(G_XK, j)
                nc.vector.tensor_copy(kx[:, j, :], banks(G_XK)[j][:, 0:NMEM]).then_inc(s_freed, 1)

            def x_max(u):
                dve.wait_ge(s_xs, u + 1)
                link(nc.vector.tensor_reduce(st_x[:, 0, u:u + 1], B[u % 4][:, 0:NMEM], mybir.AxisListType.X, ALU.max))
                nc.vector.tensor_scalar(st_x[:, 1, u:u + 1], st_x[:, 0, u:u + 1], -(XHD ** -0.5), None, ALU.mult).then_inc(s_xm, 1)

            def x_norm(u):
                dve.wait_ge(s_xe, u + 1)
                link(nc.vector.reciprocal(st_x[:, 3, u:u + 1], st_x[:, 2, u:u + 1]))
                nc.vector.tensor_scalar(px[:, u, :], px[:, u, :], st_x[:, 3, u:u + 1], None, ALU.mult).then_inc(s_xp, 1)

            for k in range(KT):
                lo(B_XK, 0, None, k, gm)
                if k == 0:
                    mem_lo(6)
                    mem_lo(7)
                if 3 <= k < 7:
                    xq_out(k - 3)
            for k in range(KT):
                lo(B_XV, 0, None, k, gm)
                if k == 2:
                    for j in range(4):
                        kx_out(j)
                for u in x_units(k - 3):
                    x_max(u)
                for u in x_units(k - 5):
                    x_norm(u)
            for u in x_units(KT - 5):
                x_norm(u)
            for k in range(XH - 1):
                lo(B_XO, 0, None, k)
            done(G_XV, 1)
            nc.vector.tensor_copy(vx[:, 0, :], banks(G_XV)[0][:, :]).then_inc(s_freed, 2)
            lo(B_XO, 0, None, XH - 1)
            for h in range(XH):
                dve.wait_ge(s_xohi, h + 1)
                nc.vector.tensor_tensor(xo_t[:, h, 1, :], B[h][:, :], xo_t[:, h, 0, :], ALU.subtract).then_inc(s_xolo, 1)

            def xo_after(n):
                t = n - 6
                if 0 <= t < KT:
                    h_sum(G_XO + t // 4, KT + t, acc[:, t, :])
                if 1 <= t < KT + 1:
                    h_part(KT + t - 1, acc[:, t - 1, :])

            for n in range(4, 16):
                lo(B_XO + n // 4 * 4, 0, None, n % 4)
                xo_after(n)
            for k in range(KT):
                lo(B_G0, 0, None, k, gf)
                xo_after(16 + k)
                if 7 <= k < 15:
                    for t in (2 * (k - 7), 2 * (k - 7) + 1):
                        add_square(KT + t, tile4[:, t % 4, :])
            rstd(2, A[0])

            def hidden_out(g, gates, n0, per=0, i=None):
                def f(j):
                    done(g, j, per, i)
                    dve.wait_ge(s_gate, gates + j + 1 + (i * 4 if i is not None else 0))
                    nc.vector.tensor_tensor(up[:, j, :], banks(g)[j][:, :], rbc[:, :], ALU.mult).then_inc(s_freed, 1)
                    out_of(g, j, per, i)
                    nc.vector.tensor_tensor(tile4[:, j, :], up[:, j, :], tile4[:, j, :], ALU.mult).then_inc(s_upp, 1)
                    dve.wait_ge(s_ahi, n0 + j + 1 + (i * 4 if i is not None else 0))
                    nc.vector.tensor_tensor(act_t[:, j, 1, :], tile4[:, j, :], act_t[:, j, 0, :], ALU.subtract).then_inc(s_alo, 1)
                return f

            def down_out(g, c, per=0, i=None):
                def f(j):
                    done(g, j, per, i)
                    t = 4 * c + j
                    nc.vector.tensor_tensor(acc[:, t, :], acc[:, t, :], banks(g)[j][:, :], ALU.add).then_inc(s_freed, 1)
                return f

            group(B_U0, KT, gf, after=gate_out(G_G0))
            with dve.Fori(0, FG - 1) as i:
                b, per = B_FFN, FFN_BLOCKS
                group(b, KT, gf, per, i, hidden_out(G_FFN - 1, 32, 0, 24, i))
                group(b + KT, 4, None, per, i, gate_out(G_FFN, 24, i))
                for c in range(1, 4):
                    group(b + KT + 4 * c, 4, None, per, i, down_out(G_FFN + c, c - 1, 24, i))
                group(b + 2 * KT, KT, gf, per, i, down_out(G_FFN + 4, 3, 24, i))
            for k in range(4):
                if k == 3:
                    hidden_out(G_LAST - 1, 32 + 4 * (FG - 1), 4 * (FG - 1))(0)
                lo(B_LAST, 0, None, k)
            for j in range(1, 4):
                hidden_out(G_LAST - 1, 32 + 4 * (FG - 1), 4 * (FG - 1))(j)

            def last_sum(t):
                g, j = G_LAST + t // 4, t % 4
                done(g, j)
                nc.vector.tensor_tensor(acc[:, t, :], acc[:, t, :], banks(g)[j][:, :], ALU.add).then_inc(s_freed, 1)

            def last_square(t):
                add_square(2 * KT + t, tile4[:, t % 4, :])

            for c in range(1, 4):
                for k in range(4):
                    lo(B_LAST + 4 * c, 0, None, k)
                for t in range(4 * c - 4, 4 * c):
                    last_sum(t)
                    if t:
                        last_square(t - 1)
            last_sum(12)
            for t in range(13, KT):
                last_sum(t)
                last_square(t - 2)
            last_square(KT - 2)
            last_square(KT - 1)
            FB = banks(G_LAST)
            rstd(3, FB[0])
            dve.wait_ge(s_gfin, 16)
            for m in range(TT * 4):
                t, kg = divmod(m, 4)
                bk = bank[(m + 1) % 8] if FB is A else bank[(m + 5) % 8]
                dve.wait_ge(s_fT, m + 1)
                f = slice(512 * kg, 512 * kg + 512)
                nc.vector.scalar_tensor_tensor(y_out[:, t, f], bk[:, :], rcol[:, t:t + 1], gfin[:, f],
                                               ALU.mult, ALU.mult).then_inc(s_y, 1)


_INS = ["x", "mem", "g_mix", "w_in", "conv_w", "sinks", "w_attn_o", "w_conv_o", "w_out", "g_xattn", "g_mem",
        "w_xq", "w_xkv", "w_xo", "g_ffn", "w_gate_up", "w_down", "g_final"]


def kernel(**inputs):
    import concourse.bacc as bacc
    from concourse.bass_utils import run_bass_kernel_spmd

    nc = bacc.Bacc("TRN2", target_bir_lowering=False, num_devices=1)
    arrays, args = {}, []
    for name in _INS:
        a = np.ascontiguousarray(inputs[name])
        arrays[f"in_{name}_dram"] = a
        args.append(nc.dram_tensor(f"in_{name}_dram", a.shape, mybir.dt.from_np(a.dtype), kind="ExternalInput").ap())
    arrays["rope_dram"] = rope_table()
    args.append(nc.dram_tensor("rope_dram", (SEQ, 2 * HALF), F32, kind="ExternalInput").ap())
    args.append(nc.dram_tensor("out_0_dram", (1, SEQ, D), F32, kind="ExternalOutput").ap())
    build(nc, *args)
    r = run_bass_kernel_spmd(nc, [arrays], core_ids=[0])
    return r.results[0]["out_0_dram"]
```
